# Optimizing a Trainium2 kernel written in Bass

```python
import math
import jax, jax.numpy as jnp
from jax import lax
import numpy as np

D_MODEL = 1024
BATCH = 1
SEQ = 512
DEPTH = 2

CHUNK = 64
N_META = 16
N_A_LAYERS = DEPTH // 2
N_B_LAYERS = DEPTH - N_A_LAYERS
S5_GROUP = 16
S5_GROUPS = D_MODEL // S5_GROUP
S5_STATE = 64
S5_MIN_STEP = 1e-3
S5_MAX_STEP = 1e-1
N_HEADS = 16
N_KV_HEADS = 4
HEAD_DIM = 64
GQ = N_HEADS // N_KV_HEADS
WINDOW = 128
WINDOW_CHUNKS = WINDOW // CHUNK
FFN_DIM = 2816
CONV_WIDTH = 3

RMS_EPS = 1e-6
NEG_INF = -1e30

kernel_name = 'yoco_s5_swa_sink_convffn_meta'

def rms_norm(x, gain):
    x32 = x.astype(jnp.float32)
    y = x32 * lax.rsqrt(jnp.mean(x32 * x32, axis=-1, keepdims=True) + RMS_EPS)
    return (y * gain.astype(jnp.float32)).astype(x.dtype)

def _ssm_combine(e1, e2):
    a1, b1 = e1
    a2, b2 = e2
    return a1 * a2, a2 * b1 + b2

def s5_mixer(u, lambda_re, lambda_im, log_step, b_re, b_im, c_re, c_im, d_skip, w_glu):
    bsz, seq_len, _ = u.shape
    f32 = jnp.float32
    u32 = u.astype(f32)
    lam = lax.complex(jnp.minimum(lambda_re.astype(f32), -1e-4), lambda_im.astype(f32))
    step = jnp.exp(log_step.astype(f32))[:, None]
    lam_bar = jnp.exp(lam * step)
    b = lax.complex(b_re.astype(f32), b_im.astype(f32))
    b_bar = ((lam_bar - 1.0) / lam)[:, :, None] * b
    c = lax.complex(c_re.astype(f32), c_im.astype(f32))
    ug = u32.reshape(bsz, seq_len, S5_GROUPS, S5_GROUP).astype(jnp.complex64)
    bu = jnp.einsum('blgh,gph->blgp', ug, b_bar)
    a = jnp.broadcast_to(lam_bar, (1, seq_len, S5_GROUPS, S5_STATE))
    _, states = lax.associative_scan(_ssm_combine, (a, bu), axis=1)
    y = jnp.einsum('blgp,ghp->blgh', states, c).real.reshape(bsz, seq_len, D_MODEL)
    y = y + d_skip.astype(f32) * u32
    g = jax.nn.gelu(y).astype(u.dtype)
    val, gate = jnp.split(g @ w_glu, 2, axis=-1)
    return val * jax.nn.sigmoid(gate)

def conv_ffn(h, w_up, conv_w, w_down):
    up = h @ w_up
    ch = up.shape[-1]
    up = lax.conv_general_dilated(up, conv_w.astype(up.dtype).reshape(CONV_WIDTH, 1, ch),
                                  window_strides=(1,), padding=[(CONV_WIDTH - 1, 0)],
                                  dimension_numbers=('NWC', 'WIO', 'NWC'),
                                  feature_group_count=ch)
    gate, val = jnp.split(up, 2, axis=-1)
    return (jax.nn.silu(gate) * val) @ w_down

def alibi_slopes():
    return jnp.exp2(-8.0 * jnp.arange(1, N_HEADS + 1, dtype=jnp.float32) / N_HEADS)

def alibi_bias(q_pos, k_pos, k_valid, slopes):
    dist = jnp.abs(q_pos[:, :, None] - k_pos[:, None, :]).astype(jnp.float32)
    bias = -slopes[None, :, :, None, None] * dist[:, None, None]
    return jnp.where(k_valid[:, None, None, None, :], bias, NEG_INF)

def sink_attend(q, k, v, bias, sink):
    f32 = jnp.float32
    s = jnp.einsum('bnqkgd,bnskd->bnkgqs', q.astype(f32), k.astype(f32)) * (HEAD_DIM ** -0.5)
    s = s + bias[None]
    sk = sink[None, None, :, :, None, None]
    m = jnp.maximum(jnp.max(s, axis=-1, keepdims=True), sk)
    p = jnp.exp(s - m)
    p = p / (jnp.sum(p, axis=-1, keepdims=True) + jnp.exp(sk - m))
    o = jnp.einsum('bnkgqs,bnskd->bnqkgd', p, v.astype(f32))
    return o.astype(q.dtype)

def chunk_band(t, n_chunks):
    bsz = t.shape[0]
    real = t[:, N_META:].reshape(bsz, n_chunks, CHUNK, N_KV_HEADS, HEAD_DIM)
    pad = jnp.pad(real, ((0, 0), (WINDOW_CHUNKS - 1, 0), (0, 0), (0, 0), (0, 0)))
    parts = [jnp.broadcast_to(t[:, None, :N_META], (bsz, n_chunks, N_META, N_KV_HEADS, HEAD_DIM))]
    parts += [pad[:, j:j + n_chunks] for j in range(WINDOW_CHUNKS)]
    return jnp.concatenate(parts, axis=2)

def window_sink_attention(hn, k, v, w_q, sinks, w_o):
    bsz, seq_len, _ = hn.shape
    n_chunks = (seq_len - N_META) // CHUNK
    q = (hn @ w_q).reshape(bsz, seq_len, N_KV_HEADS, GQ, HEAD_DIM)
    slopes = alibi_slopes().reshape(N_KV_HEADS, GQ)
    sink = sinks.astype(jnp.float32).reshape(N_KV_HEADS, GQ)
    meta_pos = jnp.arange(N_META)[None]
    bias_meta = alibi_bias(meta_pos, meta_pos, jnp.ones((1, N_META), bool), slopes)
    o_meta = sink_attend(q[:, None, :N_META], k[:, None, :N_META], v[:, None, :N_META], bias_meta, sink)
    o_meta = o_meta.reshape(bsz, N_META, N_HEADS * HEAD_DIM)
    q_blk = q[:, N_META:].reshape(bsz, n_chunks, CHUNK, N_KV_HEADS, GQ, HEAD_DIM)
    k_band = chunk_band(k, n_chunks)
    v_band = chunk_band(v, n_chunks)
    chunk_idx = jnp.arange(n_chunks)
    starts = N_META + chunk_idx * CHUNK
    frame = jnp.arange(CHUNK)
    q_pos = starts[:, None] + frame[None]
    k_pos = [jnp.broadcast_to(jnp.arange(N_META)[None], (n_chunks, N_META))]
    k_valid = [jnp.ones((n_chunks, N_META), bool)]
    for j in range(WINDOW_CHUNKS):
        off = j - (WINDOW_CHUNKS - 1)
        k_pos.append(starts[:, None] + off * CHUNK + frame[None])
        k_valid.append(jnp.broadcast_to((chunk_idx + off >= 0)[:, None], (n_chunks, CHUNK)))
    bias_real = alibi_bias(q_pos, jnp.concatenate(k_pos, axis=1), jnp.concatenate(k_valid, axis=1), slopes)
    o_real = sink_attend(q_blk, k_band, v_band, bias_real, sink)
    o_real = o_real.reshape(bsz, n_chunks * CHUNK, N_HEADS * HEAD_DIM)
    return jnp.concatenate([o_meta, o_real], axis=1) @ w_o

def shared_kv(h, kv_norm, w_kv):
    bsz, seq_len, _ = h.shape
    kv = rms_norm(h, kv_norm) @ w_kv
    k, v = jnp.split(kv, 2, axis=-1)
    return (k.reshape(bsz, seq_len, N_KV_HEADS, HEAD_DIM), v.reshape(bsz, seq_len, N_KV_HEADS, HEAD_DIM))

def setup_inputs(seed: int = 0) -> dict:
    key = jax.random.key(seed)
    ks = jax.random.split(key, 24)
    nrm = jax.random.normal
    f32 = jnp.float32
    D, F, G, P, Hc = D_MODEL, FFN_DIM, S5_GROUPS, S5_STATE, S5_GROUP
    qd, kvd = N_HEADS * HEAD_DIM, 2 * N_KV_HEADS * HEAD_DIM
    n_idx = jnp.arange(P, dtype=f32)
    return {
        'x': nrm(ks[0], (BATCH, SEQ, D), f32),
        'meta': nrm(ks[1], (N_META, D), f32),
        's5_norm': 1.0 + 0.02 * nrm(ks[2], (N_A_LAYERS, D), f32),
        's5_lambda_re': -0.5 + 0.01 * nrm(ks[3], (N_A_LAYERS, G, P), f32),
        's5_lambda_im': math.pi * n_idx + 0.01 * nrm(ks[4], (N_A_LAYERS, G, P), f32),
        's5_log_step': jax.random.uniform(ks[5], (N_A_LAYERS, G), f32, math.log(S5_MIN_STEP), math.log(S5_MAX_STEP)),
        's5_b_re': nrm(ks[6], (N_A_LAYERS, G, P, Hc), f32) * (2 * Hc) ** -0.5,
        's5_b_im': nrm(ks[7], (N_A_LAYERS, G, P, Hc), f32) * (2 * Hc) ** -0.5,
        's5_c_re': nrm(ks[8], (N_A_LAYERS, G, Hc, P), f32) * (2 * P) ** -0.5,
        's5_c_im': nrm(ks[9], (N_A_LAYERS, G, Hc, P), f32) * (2 * P) ** -0.5,
        's5_d': nrm(ks[10], (N_A_LAYERS, D), f32),
        's5_w_glu': nrm(ks[11], (N_A_LAYERS, D, 2 * D), f32) * D ** -0.5,
        'kv_norm': 1.0 + 0.02 * nrm(ks[12], (D,), f32),
        'w_kv': nrm(ks[13], (D, kvd), f32) * D ** -0.5,
        'attn_norm': 1.0 + 0.02 * nrm(ks[14], (N_B_LAYERS, D), f32),
        'w_q': nrm(ks[15], (N_B_LAYERS, D, qd), f32) * D ** -0.5,
        'sinks': 0.5 * nrm(ks[16], (N_B_LAYERS, N_HEADS), f32),
        'w_o': nrm(ks[17], (N_B_LAYERS, qd, D), f32) * qd ** -0.5,
        'ffn_norm': 1.0 + 0.02 * nrm(ks[18], (DEPTH, D), f32),
        'ffn_w_up': nrm(ks[19], (DEPTH, D, 2 * F), f32) * D ** -0.5,
        'ffn_conv': nrm(ks[20], (DEPTH, CONV_WIDTH, 2 * F), f32) * CONV_WIDTH ** -0.5,
        'ffn_w_down': nrm(ks[21], (DEPTH, F, D), f32) * F ** -0.5,
        'final_norm': 1.0 + 0.02 * nrm(ks[22], (D,), f32),
    }

def reference(x, meta, s5_norm, s5_lambda_re, s5_lambda_im, s5_log_step, s5_b_re, s5_b_im,
              s5_c_re, s5_c_im, s5_d, s5_w_glu, kv_norm, w_kv, attn_norm, w_q, sinks, w_o,
              ffn_norm, ffn_w_up, ffn_conv, ffn_w_down, final_norm):
    bsz = x.shape[0]
    h = jnp.concatenate([jnp.broadcast_to(meta.astype(x.dtype)[None], (bsz, N_META, D_MODEL)), x], axis=1)
    k_sh, v_sh = None, None
    for layer in range(DEPTH):
        if layer < N_A_LAYERS:
            i = layer
            h = h + s5_mixer(rms_norm(h, s5_norm[i]), s5_lambda_re[i], s5_lambda_im[i], s5_log_step[i],
                             s5_b_re[i], s5_b_im[i], s5_c_re[i], s5_c_im[i], s5_d[i], s5_w_glu[i])
        else:
            j = layer - N_A_LAYERS
            if j == 0:
                k_sh, v_sh = shared_kv(h, kv_norm, w_kv)
            h = h + window_sink_attention(rms_norm(h, attn_norm[j]), k_sh, v_sh, w_q[j], sinks[j], w_o[j])
        h = h + conv_ffn(rms_norm(h, ffn_norm[layer]), ffn_w_up[layer], ffn_conv[layer], ffn_w_down[layer])
    return rms_norm(h, final_norm)[:, N_META:]


_drawn_inputs = setup_inputs


def setup_inputs(seed=0):
    import zlib

    import numpy as np

    out = dict(_drawn_inputs(seed))
    spreads = {}
    factors = {'s5_norm': 5.671,
     's5_lambda_re': 8.0,
     's5_b_re': 2.898,
     's5_b_im': 2.92,
     's5_c_re': 2.888,
     's5_c_im': 2.876,
     'kv_norm': 8.0,
     'attn_norm': 8.0,
     'sinks': 4.288,
     'ffn_norm': 2.784,
     'final_norm': 2.825}
    for name, (base, spread) in spreads.items():
        noise = np.random.default_rng([zlib.crc32(name.encode()), seed]).standard_normal(out[name].shape)
        drawn = base * np.exp(spread * noise) if base else spread * noise
        out[name] = __import__('jax').numpy.asarray(drawn.astype(out[name].dtype))
    for name, factor in factors.items():
        out[name] = (out[name] * factor).astype(out[name].dtype)
    return out
```

```python
from contextlib import ExitStack

import numpy as np

import concourse.bass as bass
from concourse import mybir

F32 = mybir.dt.float32
F32R = mybir.dt.float32r
I32 = mybir.dt.int32
ACT = mybir.ActivationFunctionType
ALU = mybir.AluOpType
AX = mybir.AxisListType

P = 128
D = 1024
SEQ = 512
META = 16
L = SEQ + META
HALF = L // 2
KD = D // P
FFN = 2816
KF = FFN // P
EPS = 1e-6
G, S, HC = 64, 64, 16
T = 8
NC = L // T
PAIRS = G // 2
TH = T * HC
CH = 64
NCH = SEQ // CH
NQ = NCH + 1
BAND = 2 * CH
KEYS = BAND + META
HD = 64
HEADS = 16
KVH = 4
HP = HEADS // 2
Q_CUT = META + SEQ // 2
GRP = 3
FAR = 1e30
MAGIC = 1.5 * 2.0 ** 23

S_GLU = 0
S_UP0 = S_GLU + 2 * KD
S_DN0 = S_UP0 + 2 * KF
S_KV = S_DN0 + 2 * KD
S_Q = S_KV + 4
S_O = S_Q + KD
S_UP1 = S_O + KD
S_DN1 = S_UP1 + 2 * KF
S_END = S_DN1 + 2 * KD
KS = KF // 2


class Chain:

    def __init__(self, eng, sem):
        self.eng, self.sem, self.base, self.moving, self.k = eng, sem, 0, None, 0

    def did(self, ins):
        self.k += 1
        ins.then_inc(self.sem, 1)
        return self.value()

    def value(self):
        v = self.base + self.k
        return v if self.moving is None else self.moving + v

    def wait(self, value):
        self.eng.wait_ge(self.sem, value)

    def sync(self):
        self.eng.wait_ge(self.sem, self.value())

    def link(self, ins):
        self.did(ins)
        self.sync()

    def loop(self, i, per):
        self.base, self.k = self.base + self.k - per, 0
        self.moving = self.eng.snap(i * per)

    def leave(self, n, per):
        assert self.k == per, (self.k, per)
        self.base, self.k, self.moving = self.base + per * (n + 1), 0, None


def trunk(nc, x, meta, s5_norm, s5_lambda_re, s5_lambda_im, s5_log_step, s5_b_re, s5_b_im, s5_c_re, s5_c_im,
          s5_d, s5_w_glu, kv_norm, w_kv, attn_norm, w_q, sinks, w_o, ffn_norm, ffn_w_up, ffn_conv, ffn_w_down,
          final_norm, out, k_scratch, v_scratch):

    first = (nc.sbuf_base + 31) // 32 * 8
    last = nc.sbuf_usable_end // 4

    def at(name, col, cols, dtype=F32):
        assert first + col + cols <= last, name
        return nc.alloc_sbuf_tensor_at(name, [P, cols], dtype, offset=4 * (first + col))

    class Zone:

        def __init__(self, col, cols):
            self.col, self.end = col, col + cols

        def put(self, name, cols, dtype=F32):
            assert self.col + cols <= self.end, (name, self.col + cols - self.end)
            t = at(name, self.col, cols, dtype)
            self.col += (cols + 7) // 8 * 8
            return t

    W_RAW, W_SPL = 2 * KS * P, 4 * KS * P
    Z_K = 0
    Z_H = Z_K + 616
    Z_RAW = Z_H + KD * L
    Z_SPL = Z_RAW + W_RAW
    Z_A = Z_SPL + W_SPL
    Z_B = Z_A + 2 * KD * L
    Z_C = Z_B + 2 * KF * L
    C_COLS = last - first - Z_C

    z = Zone(Z_K, Z_H - Z_K)
    ident = z.put("ident", P)
    ones = z.put("ones", P)
    gains = z.put("gains", 5 * KD)
    conv_w = z.put("conv_w", 2 * 3 * 2 * KF)
    negslope = z.put("negslope", HP)
    sink = z.put("sink", HP)
    eps = z.put("eps", 1)
    gain = lambda g: gains[:, g * KD:(g + 1) * KD]
    G_FFN = [0, 3]
    G_KV, G_ATT, G_FIN = 1, 2, 4
    cw = conv_w[:].rearrange("p (l t m) -> p l t m", l=2, t=3)

    h = at("h", Z_H, KD * L)[:].rearrange("p (k n) -> p k n", k=KD)
    raw = at("raw", Z_RAW, W_RAW)[:].rearrange("p (b c) -> p b c", b=2)
    zs = Zone(Z_SPL, W_SPL)
    w_hi = zs.put("w_hi", W_SPL // 2, F32R)[:].rearrange("p (b c) -> p b c", b=2)
    w_lo = zs.put("w_lo", W_SPL // 2, F32R)[:].rearrange("p (b c) -> p b c", b=2)
    tiles = lambda t, n: t[:].rearrange("p (k n) -> p k n", k=n)
    za = Zone(Z_A, 2 * KD * L)
    xa_hi = tiles(za.put("xa_hi", KD * L, F32R), KD)
    xa_lo = tiles(za.put("xa_lo", KD * L, F32R), KD)
    zb = Zone(Z_B, 2 * KF * L)
    act_hi = tiles(zb.put("act_hi", KF * L, F32R), KF)
    act_lo = tiles(zb.put("act_lo", KF * L, F32R), KF)
    f32 = lambda ap: ap.bitcast(F32)

    def tile_of(t, m, a=0, b=L):
        return t[:, m, a:b] if isinstance(m, int) else t[:, bass.ds(m, 1), a:b].rearrange("p a n -> p (a n)")

    def column(t, m):
        return t[:, m:m + 1] if isinstance(m, int) else t[:, bass.ds(m, 1)]

    za = Zone(Z_A, 2 * KD * L)
    xc = za.put("xc", T * D)
    za = Zone(Z_A, 2 * KD * L)
    xt = za.put("xt", 5 * D)
    zb = Zone(Z_B, 2 * KF * L)
    u5 = zb.put("u5", G * NC)[:].rearrange("p (g c) -> p g c", g=G)
    cpow = [zb.put(f"cpow{r}", PAIRS * (T + 1) * HC)[:].rearrange("p (q k h) -> p q k h", q=PAIRS, k=T + 1)
            for r in range(2)]
    toep = zb.put("toep", G * TH)[:].rearrange("p (g c) -> p g c", g=G)
    xn = at("xn", Z_B + G * NC + 2 * PAIRS * (T + 1) * HC, G * TH)[:].rearrange(
        "p (g t h) -> p g t h", g=G, t=T)
    dtmp = [zb.put(f"dtmp{n}", 512) for n in range(2)]
    ptmp = zb.put("ptmp", 4 * (T + 1) * HC)
    zc = Zone(Z_C, C_COLS)
    zst = zc.put("zst", 2 * PAIRS * NC)[:].rearrange("p (q r c) -> p q r c", q=PAIRS, r=2)
    gy = zc.put("gy", 2 * T * P)[:].rearrange("p (b t c) -> p b t c", b=2, t=T)
    lpow = [zc.put(f"lpow{r}", PAIRS * (T + 1))[:].rearrange("p (k q) -> p k q", k=T + 1) for r in range(2)]
    coef = [zc.put(f"coef{r}", PAIRS) for r in range(2)]
    l8a = zc.put("l8a", 2 * PAIRS)[:].rearrange("p (q r) -> p q r", r=2)
    l8b = zc.put("l8b", 2 * PAIRS)[:].rearrange("p (q r) -> p q r", r=2)
    st1 = zc.put("st1", 2 * PAIRS)[:].rearrange("p (q r) -> p q r", r=2)
    st2 = zc.put("st2", 2 * PAIRS)[:].rearrange("p (q r) -> p q r", r=2)
    gain5 = zc.put("gain5", G)
    ssq5 = zc.put("ssq5", T)
    rst5 = zc.put("rst5", T)
    zpad = at("zpad", Z_B + G * NC + 2 * PAIRS * (T + 1) * HC + G * TH, 3 * 8 * NC)[:].rearrange(
        "p (u q g r c) -> p u q g r c", u=3, q=2, g=2, r=2)
    zp = Zone(Z_C, 2 * PAIRS * NC)
    pm = {n: zp.put("pm_" + n, P) for n in ("lr", "li", "ar", "ai", "r", "th", "n", "s", "c", "a", "b", "d",
                                            "lbr", "lbi", "cr", "ci")}
    pi = zp.put("pm_int", P, I32)
    lst = zp.put("lst", 2)
    stp = zp.put("stp", 2)
    se = {n: zp.put("se_" + n, 2) for n in ("a", "b", "c", "d")}
    sei = zp.put("se_int", 2, I32)
    g5row = zp.put("g5row", TH)
    grow = zp.put("grow", P)
    crow = zp.put("crow", 3 * P)
    sinkrow = zp.put("sinkrow", HEADS)
    zh = Zone(Z_H, KD * L)
    win_t = zh.put("win_t", 2 * 2 * 4 * TH)[:].rearrange("p (b r q t h) -> p b r q t h", b=2, r=2, q=4, t=T)
    win = zh.put("win", 2 * 2 * 4 * P)[:].rearrange("p (b r q s) -> p b r q s", b=2, r=2, q=4)
    zr = Zone(Z_RAW, W_RAW)
    bbar = [zr.put(f"bbar{r}", PAIRS * HC)[:].rearrange("p (q h) -> p q h", q=PAIRS) for r in range(2)]
    dskip = zr.put("dskip", PAIRS * HC)[:].rearrange("p (q h) -> p q h", q=PAIRS)
    drow = zr.put("drow", PAIRS * HC)[:].rearrange("p (q h) -> p q h", q=PAIRS)
    diag2 = zr.put("diag2", HC)
    zs = Zone(Z_SPL, W_SPL)
    braw = [zs.put(f"braw{r}", PAIRS * HC)[:].rearrange("p (q h) -> p q h", q=PAIRS) for r in range(2)]
    craw = [zs.put(f"craw{r}", KD * 2 * S)[:].rearrange("p (r t s) -> p r t s", r=KD, t=2) for r in range(2)]
    zs = Zone(Z_SPL, W_SPL)
    kern = zs.put("kern", 2 * 8 * TH)[:].rearrange("p (b q c) -> p b q c", b=2, q=8)
    zs = Zone(Z_SPL + 4 * TH * 7, W_SPL - 4 * TH * 7)
    bpad = [zs.put(f"bpad{r}", PAIRS * 2 * HC)[:].rearrange("p (q g h) -> p q g h", q=PAIRS, g=2) for r in range(2)]

    zc = Zone(Z_C, C_COLS)
    rinv = zc.put("rinv", L)
    rinv8 = zc.put("rinv8", L)
    acc = zc.put("acc", L)
    sq = tiles(zc.put("sq", 2 * L), 2)
    ubuf = tiles(zc.put("ubuf", 2 * (L + 2)), 2)
    cbuf = tiles(zc.put("cbuf", 2 * L), 2)
    abuf = zc.put("abuf", L)
    sig = tiles(zc.put("sig", 2 * L), 2)
    dist = zc.put("dist", NQ * KEYS)[:].rearrange("p (n j) -> p n j", n=NQ)
    vcur = zc.put("vcur", NCH * HD)[:].rearrange("p (n d) -> p n d", n=NCH)
    zc = Zone(Z_C + 3 * L + 2 * L, 2 * (L + 2) + 2 * L + L)
    mneg = tiles(zc.put("mneg", 2 * NQ), 2)
    den = tiles(zc.put("den", 2 * NQ), 2)
    esnk = tiles(zc.put("esnk", 2 * NQ), 2)
    rden = tiles(zc.put("rden", 2 * NQ), 2)
    dint = zc.put("dint", KEYS * NQ, I32)
    zb = Zone(Z_B, 2 * KF * L)
    xq_hi = tiles(zb.put("xq_hi", KD * L, F32R), KD)
    xq_lo = tiles(zb.put("xq_lo", KD * L, F32R), KD)
    ao_hi = tiles(zb.put("ao_hi", KD * L, F32R), KD)
    ao_lo = tiles(zb.put("ao_lo", KD * L, F32R), KD)
    kvt = tiles(zb.put("kvt", 4 * L), 4)
    vtok = zb.put("vtok", 5 * 2 * P)[:].rearrange("p (n c) -> p n c", n=5)
    za = Zone(Z_A, 2 * KD * L)
    qt = za.put("qt", 2 * NQ * P)[:].rearrange("p (e n x f) -> p e n x f", e=2, n=NQ, x=2)
    kcur = za.put("kcur", NQ * KEYS)[:].rearrange("p (n j) -> p n j", n=NQ)
    prob = za.put("prob", 2 * NQ * KEYS)[:].rearrange("p (b n j) -> p b n j", b=2, n=NQ)
    probm = za.put("probm", 2 * NQ * META)[:].rearrange("p (b n j) -> p b n j", b=2, n=NQ)
    pt = za.put("pt", NQ * P)[:].rearrange("p (n q) -> p n q", n=NQ)
    ptm = za.put("ptm", GRP * P)[:].rearrange("p (t q) -> p t q", t=GRP)
    vmet = za.put("vmet", GRP * HD)[:].rearrange("p (n d) -> p n d", n=GRP)
    za = Zone(Z_A, 2 * KD * L)
    otok = za.put("otok", 4 * D)[:].rearrange("p (n c) -> p n c", n=4)

    up_v = [ffn_w_up[l].rearrange("(k p) c -> p k c", p=P) for l in range(2)]
    dn_v = [ffn_w_down[l].rearrange("(k p) c -> p k c", p=P) for l in range(2)]
    glu_v = s5_w_glu[0].rearrange("(k p) c -> p k c", p=P)
    kv_v = w_kv.rearrange("(k p) c -> p k c", p=P)
    q_v = w_q[0].rearrange("(k p) c -> p k c", p=P)
    o_v = w_o[0].rearrange("(k p) c -> p k c", p=P)

    ctx = ExitStack()
    with ctx:
        sem = lambda name: ctx.enter_context(nc.semaphore(name))
        slot = [ctx.enter_context(nc.psum_tensor(f"slot{n}", [P, 2, 512], F32)) for n in range(4)]
        acc_of = lambda n: slot[n][:, :, 0:HALF]
        halves = lambda ap: ap.rearrange("p (a n) -> p a n", a=2)

        raw_landed = [sem("raw_landed0"), sem("raw_landed1")]
        hi_done, lo_done, slab_used = sem("hi_done"), sem("lo_done"), sem("slab_used")
        act_chain, dve_chain, pool_chain = sem("act_chain"), sem("dve_chain"), sem("pool_chain")

        consts_set, x_in, par_in, rows_in, b_in, c_in, g5_in, d_in, xt_in = (
            sem(n) for n in ("consts_set", "x_in", "par_in", "rows_in", "b_in", "c_in", "g5_in", "d_in", "xt_in"))
        angles_ready, sincos_ready, par_ready, ssq5_ready, rst5_ready, xn_ready = (
            sem(n) for n in ("angles_ready", "sincos_ready", "par_ready", "ssq5_ready", "rst5_ready", "xn_ready"))
        s5_full = sem("s5_full")
        s5_free = [sem(f"s5_free{n}") for n in range(4)]
        lpow_ready, cpow_ready, dskip_ready, toep_zero = (
            sem(n) for n in ("lpow_ready", "cpow_ready", "dskip_ready", "toep_zero"))
        win_t_ready, scan_done, kern_d_ready = (sem(n) for n in ("win_t_ready", "scan_done", "kern_d_ready"))
        bpad_ready, zpad_zero, zpad_ready, zpad_used = (
            sem(n) for n in ("bpad_ready", "zpad_zero", "zpad_ready", "zpad_used"))
        toep_in = [sem(f"toep_in{b}") for b in range(4)]
        glu_x_hi = sem("glu_x_hi")
        glu_sig, glu_mul, ubuf_zero = sem("glu_sig"), sem("glu_mul"), sem("ubuf_zero")
        RES = ("glu", "dn0", "o", "dn1")
        h_done, sq_done, acc_zero, acc_done, x_hi_done, x_lo_done = (
            {p: sem(f"{n}_{p}") for p in RES} for n in ("h_done", "sq_done", "acc_zero", "acc_done", "x_hi_done",
                                                        "x_lo_done"))
        stat_full, stat_read, rinv_ready = (
            {p: sem(f"{n}_{p}") for p in ("glu", "dn0", "o")} for n in ("stat_full", "stat_read", "rinv_ready"))
        UPS = ("up0", "up1")
        up_evicted, tap_done, conv_gate, silu_done, act_done, act_hi_done, act_lo_done = (
            {p: sem(f"{n}_{p}") for p in UPS} for n in ("up_evicted", "tap_done", "conv_gate", "silu_done", "act_done",
                                                        "act_hi_done", "act_lo_done"))
        dint_set, dist_abs, dist_set, pads_zero = (sem(n) for n in ("dint_set", "dist_abs", "dist_set", "pads_zero"))
        kv_evicted, v_full, v_copied, kv_written, k_in, v_in = (
            sem(n) for n in ("kv_evicted", "v_full", "v_copied", "kv_written", "k_in", "v_in"))
        xq_hi_done, xq_lo_done, q_evicted, scores_done, m_ready, exp_done, rden_ready, p_ready = (
            sem(n) for n in ("xq_hi_done", "xq_lo_done", "q_evicted", "scores_done", "m_ready", "exp_done",
                             "rden_ready", "p_ready"))
        pt_full, pt_copied, pv_done, ao_hi_done, ao_lo_done = (
            sem(n) for n in ("pt_full", "pt_copied", "pv_done", "ao_hi_done", "ao_lo_done"))
        hg_done, ot_full, ot_copied, fin_full, fin_rms, fin_rinv, scaled_act, scaled_dve, written = (
            sem(n) for n in ("hg_done", "ot_full", "ot_copied", "fin_full", "fin_rms", "fin_rinv", "scaled_act",
                             "scaled_dve", "written"))

        block = ctx.enter_context(nc.Block())

        fills = (["par", "c0", "c1"] + [f"u{b}" for b in range(8)]
                 + [name for b in range(8) for name in (f"w{b}", f"v{b}")]
                 + [f"g{b}" for b in range(4)] + [f"h{k}" for k in range(KD)]
                 + ["y0"] + [name for k in range(1, KD) for name in (f"y{k}", f"t{k - 1}")] + [f"t{KD - 1}"])
        fill_of = {name: n for n, name in enumerate(fills)}
        fslot = lambda name: slot[fill_of[name] % 4]
        N_FILLS = [len([n for n in range(len(fills)) if n % 4 == k]) for k in range(4)]

        def full_wait(eng, name):
            eng.wait_ge(s5_full, fill_of[name] + 1)

        def copied_wait(eng, name):
            n = fill_of[name]
            eng.wait_ge(s5_free[n % 4], n // 4 + 1)

        def frees(ins, name):
            ins.then_inc(s5_free[fill_of[name] % 4], 1)

        @block.sync
        def _(sp):
            dma = sp.dma_start
            dma(pm["lr"][0:PAIRS, :], s5_lambda_re[0].rearrange("(q t) s -> q (t s)", t=2)).then_inc(par_in, 16)
            dma(pm["li"][0:PAIRS, :], s5_lambda_im[0].rearrange("(q t) s -> q (t s)", t=2)).then_inc(par_in, 16)
            dma(lst[0:PAIRS, :], s5_log_step[0].rearrange("(q t) -> q t", t=2)).then_inc(par_in, 16)
            dma(xc[0:2, :], meta.rearrange("(c t) d -> c (t d)", t=T)).then_inc(x_in, 16)
            dma(xc[2:NC, :], x[0].rearrange("(c t) d -> c (t d)", t=T)).then_inc(x_in, 16)
            for t in range(T):
                dma(g5row[0:G, t * HC:(t + 1) * HC], s5_norm[0].rearrange("(g h) -> g h", g=G)).then_inc(g5_in, 16)
            for n, g in enumerate((ffn_norm[0], kv_norm, attn_norm[0], ffn_norm[1], final_norm)):
                dma(grow[n * KD:(n + 1) * KD, :], g.rearrange("(k p) -> k p", p=P)).then_inc(rows_in, 16)
            dma(crow[0:4 * KF, :].rearrange("q (r p) -> q r p", r=3),
                ffn_conv.rearrange("l t (m p) -> (l t m) p", p=P).rearrange("(r q) p -> q r p", r=3)
                ).then_inc(rows_in, 16)
            dma(sinkrow[:, :], sinks[0].partition_broadcast(P)).then_inc(rows_in, 16)
            for r, b in enumerate((s5_b_re, s5_b_im)):
                dma(braw[r], b[0].rearrange("(q t) s h -> (t s) q h", t=2)).then_inc(b_in, 16)
            for r, c in enumerate((s5_c_re, s5_c_im)):
                for t in range(2):
                    dma(craw[r][:, :, t, :],
                        c[0].rearrange("g h s -> (g h) s").rearrange("(r q) s -> q r s", r=KD)).then_inc(c_in, 16)
            for g2 in range(2):
                dma(drow[g2 * HC:(g2 + 1) * HC], s5_d[0].rearrange("(q g h) -> g q h", g=2, h=HC)[g2].partition_broadcast(HC)
                    ).then_inc(d_in, 16)
            full_wait(sp, "u7")
            dma(xt[:, 0:4 * D].rearrange("p (n d) -> p n d", n=4), x[0].rearrange("(n p) d -> p n d", p=P)
                ).then_inc(xt_in, 16)
            dma(xt[0:META, 4 * D:5 * D], meta).then_inc(xt_in, 16)
            sp.wait_ge(toep_zero, 1)
            for b in range(4):
                sp.wait_ge(kern_d_ready, b + 1)
                for t in range(T):
                    for g2 in range(2):
                        dma(toep[t * HC:(t + 1) * HC, 16 * b:16 * (b + 1), t * HC:TH].rearrange(
                                "p (q g) c -> p q g c", g=2)[:, :, g2],
                            kern[g2 * HC:(g2 + 1) * HC, b % 2, :, 0:TH - t * HC]).then_inc(toep_in[b], 16)

            def load(buf, src, nk, split):
                if split is not None:
                    sp.wait_ge(hi_done, split)
                    sp.wait_ge(lo_done, split)
                dma(raw[:, buf, 0:nk * P].rearrange("p (k c) -> p k c", k=nk), src).then_inc(raw_landed[buf], 16)

            load(0, glu_v[:, :, 0:P], KD, None)
            load(1, glu_v[:, :, D:D + P], KD, None)
            load(0, glu_v[:, :, P:2 * P], KD, 1)
            load(1, glu_v[:, :, D + P:D + 2 * P], KD, 2)

            def two_streams(w, start, turns, other, base):
                with sp.Fori(start, turns) as i:
                    cols = [sp.snap(i * (2 * P) + c) for c in (0, other, P, other + P)]
                    split = [sp.snap(i * 4 + (base + n - 1)) for n in range(4)]
                    for n in range(4):
                        load(n % 2, w[:, :, bass.ds(cols[n], P)], KD, split[n])

            def down(w, base):
                with sp.Fori(0, KD) as i:
                    col = sp.snap(i * P)
                    split = [sp.snap(i * 2 + (base + n - 1)) for n in range(2)]
                    for n in range(2):
                        load(n, w[:, n * KS:(n + 1) * KS, bass.ds(col, P)], KS, split[n])

            def one_stream(w, tiles, base):
                with sp.Fori(0, tiles // 2) as i:
                    cols = [sp.snap(i * (2 * P) + n * P) for n in range(2)]
                    split = [sp.snap(i * 2 + (base + n - 1)) for n in range(2)]
                    for n in range(2):
                        load(n, w[:, :, bass.ds(cols[n], P)], KD, split[n])

            two_streams(glu_v, 1, KD // 2, D, S_GLU)
            two_streams(up_v[0], 0, KF // 2, FFN, S_UP0)
            down(dn_v[0], S_DN0)
            one_stream(kv_v, 4, S_KV)
            for n in range(2):
                load(n, q_v[:, :, n * P:(n + 1) * P], KD, S_Q + n - 1)
            for a in range(2):
                sp.wait_ge(kv_evicted, a + 1)
                dma(k_scratch[2 * a:2 * a + 2].rearrange("t d n -> (t d) n"), kvt[:, a, :]).then_inc(kv_written, 16)
            sp.wait_ge(v_copied, 2)
            dma(v_scratch[META:L, :].rearrange("(n p) c -> p n c", p=P), vtok[:, 0:4, :]).then_inc(kv_written, 16)
            dma(v_scratch[0:META, :], vtok[0:META, 4, :]).then_inc(kv_written, 16)
            sp.wait_ge(kv_written, 64)
            sp.wait_ge(pads_zero, 1)

            def kv_load(j, j64, scored, used):
                kj = k_scratch[bass.ds(j, 1)].rearrange("a d n -> (a d) n") if not isinstance(j, int) else k_scratch[j]
                if scored is not None:
                    sp.wait_ge(scores_done, scored)
                for half in range(2):
                    rows = slice(half * CH, (half + 1) * CH)
                    dma(kcur[rows, 1:NCH, 0:CH],
                        kj[:, META:L - CH].rearrange("d (n f) -> d n f", f=CH)).then_inc(k_in, 16)
                    dma(kcur[rows, 0:NCH, CH:BAND],
                        kj[:, META:L].rearrange("d (n f) -> d n f", f=CH)).then_inc(k_in, 16)
                    dma(kcur[rows, :, BAND:KEYS],
                        kj[:, None, 0:META].to_broadcast([HD, NQ, META])).then_inc(k_in, 16)
                if used is not None:
                    sp.wait_ge(pv_done, used)
                vj = v_scratch[:, bass.ds(j64, HD)]
                dma(vcur[0:CH, 1:NCH, :], vj[META:L - CH, :].rearrange("(n f) d -> f n d", f=CH)).then_inc(v_in, 16)
                dma(vcur[CH:P, 0:NCH, :], vj[META:L, :].rearrange("(n f) d -> f n d", f=CH)).then_inc(v_in, 16)
                for n in range(GRP):
                    dma(vmet[n * META:(n + 1) * META, n, :], vj[0:META, :]).then_inc(v_in, 16)

            kv_load(0, 0, None, None)
            with sp.Fori(1, KVH) as j:
                j64, scored, used = sp.snap(j * HD), sp.snap(j * (2 * GRP)), sp.snap(j * 2)
                jr = sp.snap(j * 1)
                cols = [sp.snap(j * (2 * P) + n * P) for n in range(2)]
                split = [sp.snap(j * 2 + (S_Q + n - 1)) for n in range(2)]
                for n in range(2):
                    load(n, q_v[:, :, bass.ds(cols[n], P)], KD, split[n])
                kv_load(jr, j64, scored, used)
            one_stream(o_v, KD, S_O)
            two_streams(up_v[1], 0, KF // 2, FFN, S_UP1)
            down(dn_v[1], S_DN1)
            for n in range(4):
                sp.wait_ge((scaled_act, scaled_dve)[n % 2], n // 2 + 1)
                dma(out[0, n * P:(n + 1) * P, :], otok[:, n, :]).then_inc(written, 16)
            sp.wait_ge(written, 64)

        @block.scalar
        def _(act):
            chain = Chain(act, act_chain)
            run = nc.scalar.activation

            def split(s, buf, raw_count, nk):
                act.wait_ge(raw_landed[buf], raw_count)
                act.wait_ge(slab_used, s - 1)
                run(w_hi[:, buf, 0:nk * P], raw[:, buf, 0:nk * P], ACT.Copy).then_inc(hi_done, 1)

            def landed(buf, s):
                return 8 * (s - buf) + 16

            def split_at(base, m, per, q, nk):
                buf = (base + q) % 2
                split(m * per + (base + q), buf, m * (8 * per) + landed(buf, base + q), nk)

            act.wait_ge(angles_ready, 1)
            run(pm["s"][0:PAIRS, :], pm["a"][0:PAIRS, :], ACT.Sin)
            run(pm["c"][0:PAIRS, :], pm["b"][0:PAIRS, :], ACT.Sin).then_inc(sincos_ready, 1)
            act.wait_ge(x_in, 32)
            act.wait_ge(consts_set, 1)
            junk = win_t[0:NC].rearrange("p b r q t h -> p (b r q t h)")
            for t in range(T):
                if t >= 2:
                    chain.wait(chain.value() - 1)
                chain.did(run(junk[:, (t % 2) * D:(t % 2 + 1) * D], xc[0:NC, t * D:(t + 1) * D], ACT.Square,
                              accum_out=ssq5[0:NC, t:t + 1]))
            chain.sync()
            run(ssq5[0:NC, :], ssq5[0:NC, :], ACT.Sqrt, scale=1.0 / D, bias=eps[0:NC, :]).then_inc(ssq5_ready, 1)
            act.wait_ge(rst5_ready, 1)
            for t in range(T):
                run(xn[0:NC, :, t, :], xc[0:NC, t * D:(t + 1) * D].rearrange("c (g h) -> c g h", g=G), ACT.Copy,
                    scale=rst5[0:NC, t:t + 1]).then_inc(xn_ready, 1)
            for r in range(2):
                name = f"c{r}"
                full_wait(act, name)
                for t in range(2):
                    part = slice(t * S, (t + 1) * S)
                    ins = run(cpow[r][part, :, 0, :].rearrange("p (b x) h -> p b x h", b=2),
                              fslot(name)[part, :, :].rearrange("p b (x t h) -> p b x t h", t=2, h=HC)[:, :, :, t, :],
                              ACT.Copy, scale=(1.0, -1.0)[r])
                frees(ins, name)
            for b in range(8):
                name = f"w{b}"
                full_wait(act, name)
                ins = run(win[:, b % 2].rearrange("p r q s -> p r (q s)"), fslot(name)[:, :, :], ACT.Copy)
                frees(ins, name)
            for b in range(4):
                name = f"g{b}"
                full_wait(act, name)
                if b >= 2:
                    act.wait_ge(toep_in[b - 2], 32 * T)
                frees(run(kern[0:2 * HC, b % 2].rearrange("p (a q) c -> p a (q c)", a=2), fslot(name)[0:2 * HC, :, :],
                          ACT.Copy), name)
            for k in range(KD):
                name = f"h{k}"
                full_wait(act, name)
                run(h[:, k, 0:META + 2 * P], fslot(name)[:, 0, 0:META + 2 * P], ACT.Copy)
                frees(run(h[:, k, META + 2 * P:L], fslot(name)[:, 1, 0:2 * P], ACT.Copy), name)

            def glu_operand(k):
                name = f"t{k}"
                full_wait(act, name)
                for half in range(2):
                    ins = run(xa_hi[:, k, :].rearrange("p (c b t) -> p b t c", b=2, t=T // 2)[:, half],
                              fslot(name)[:, half, 0:4 * NC].rearrange("p (t c) -> p t c", t=4), ACT.Copy)
                ins.then_inc(glu_x_hi, 1)

            for k in range(KD):
                name = f"y{k}"
                full_wait(act, name)
                if k >= 2:
                    full_wait(act, f"t{k - 2}")
                for half in range(2):
                    ins = run(gy[0:NC, k % 2].rearrange("c t (b g h) -> c b g t h", b=2, h=HC)[:, half],
                              fslot(name)[0:NC, half, :].rearrange("p (g t h) -> p g t h", g=4, t=T),
                              ACT.Gelu_apprx_tanh)
                frees(ins, name)
                if k == 0:
                    for b in range(4):
                        act.wait_ge(toep_in[b], 32 * T)
                    act.wait_ge(raw_landed[0], 16)
                    run(w_hi[:, 0, 0:KD * P], raw[:, 0, 0:KD * P], ACT.Copy).then_inc(hi_done, 1)
                if k >= 1:
                    glu_operand(k - 1)
            glu_operand(KD - 1)

            def residual(p, m, par, g):
                act.wait_ge(h_done[p], m + 1)
                if not isinstance(m, int) or m >= 2:
                    act.wait_ge(acc_done[p], m - 1)
                run(sq[:, par, :], tile_of(h, m), ACT.Square).then_inc(sq_done[p], 1)
                if g is not None:
                    mi = m if isinstance(m, int) else act.snap(m)
                    run(tile_of(xa_hi, mi), tile_of(h, mi), ACT.Copy, scale=column(gain(g), mi)
                        ).then_inc(x_hi_done[p], 1)

            def rms(p):
                act.wait_ge(stat_full[p], 1)
                run(halves(rinv[:, :]), acc_of(3), ACT.Sqrt, scale=1.0 / D, bias=eps[:, :]).then_inc(stat_read[p], 1)

            def gate(m, par):
                act.wait_ge(slab_used, m * 2 + (S_GLU + 2))
                if not isinstance(m, int) or m >= 2:
                    act.wait_ge(h_done["glu"], m - 1)
                run(halves(sig[:, par, :]), acc_of(2 * par + 1), ACT.Sigmoid).then_inc(glu_sig, 1)

            def glu_tile(m, par, nxt=KD):
                if isinstance(m, int) and m == 0:
                    act.wait_ge(raw_landed[1], 16)
                    run(w_hi[:, 1, 0:KD * P], raw[:, 1, 0:KD * P], ACT.Copy).then_inc(hi_done, 1)
                else:
                    split_at(S_GLU, m, 2, 1, KD)
                    gate(m - 1, 1 - par)
                    residual("glu", m - 1, 1 - par, None)
                split_at(S_GLU, m, 2, 2, nxt)

            glu_tile(0, 0)
            glu_tile(1, 1)
            with act.Fori(1, KD // 2) as i:
                for e in range(2):
                    glu_tile(act.snap(i * 2 + e), e)
            gate(KD - 1, 1)
            residual("glu", KD - 1, 1, None)

            def up(p, l, base, before, nxt):
                def tap(q, m):
                    act.wait_ge(up_evicted[p], m * 2 + (q + 1))
                    if not isinstance(m, int) or m >= 1:
                        act.wait_ge(act_done[p], m)
                    w = column(cw[:, l, 2, :], q * KF + m if isinstance(m, int) else act.snap(m + q * KF))
                    run(cbuf[:, q, :], ubuf[:, q, 2:L + 2], ACT.Copy, scale=w).then_inc(tap_done[p], 1)

                def gate_tile(m):
                    tap(0, m)
                    act.wait_ge(conv_gate[p], m + 1)
                    run(cbuf[:, 0, :], cbuf[:, 0, :], ACT.Silu).then_inc(silu_done[p], 1)

                def val_tile(m):
                    tap(1, m)
                    act.wait_ge(act_done[p], m + 1)
                    run(tile_of(act_hi, m), abuf[:, :], ACT.Copy).then_inc(act_hi_done[p], 1)

                def tile(m, n2):
                    split_at(base, m, 2, 1, KD)
                    if isinstance(m, int) and m == 0:
                        rms(before)
                    else:
                        val_tile(m - 1 if isinstance(m, int) else act.snap(m - 1))
                    split_at(base, m, 2, 2, n2)
                    gate_tile(m)

                tile(0, KD)
                tile(1, KD)
                with act.Fori(1, KF // 2 - 1) as i:
                    for e in range(2):
                        tile(act.snap(i * 2 + e), KD)
                tile(KF - 2, KD)
                tile(KF - 1, KS)
                val_tile(KF - 1)

            def down(p, base, g, nxt):
                def tile(m, par, n2):
                    split_at(base, m, 2, 1, KS)
                    if not (isinstance(m, int) and m == 0):
                        residual(p, m - 1 if isinstance(m, int) else act.snap(m - 1), 1 - par, g)
                    elif p == "dn0":
                        act.wait_ge(dint_set, 2)
                        run(dist[:, :, :], dint[:, :].rearrange("p (n j) -> p n j", n=NQ), ACT.Abs
                            ).then_inc(dist_abs, 1)
                    if n2:
                        split_at(base, m, 2, 2, n2)
                    if p == "dn1" and not (isinstance(m, int) and m == 0):
                        out_copy(m - 1 if isinstance(m, int) else act.snap(m - 1), 1 - par)

                tile(0, 0, KS)
                tile(1, 1, KS)
                with act.Fori(1, KD // 2 - 1) as i:
                    for e in range(2):
                        tile(act.snap(i * 2 + e), e, KS)
                tile(KD - 2, 0, KS)
                tile(KD - 1, 1, nxt)
                residual(p, KD - 1, 1, g)
                if p == "dn1":
                    out_copy(KD - 1, 1)

            def out_copy(m, par):
                act.wait_ge(ot_full, m + 1)
                o = otok[:, :, m * P:(m + 1) * P] if isinstance(m, int) else otok[:, :, bass.ds(act.snap(m * P), P)]
                run(o, slot[2 + par][:, 0, :].rearrange("p (n c) -> p n c", n=4), ACT.Copy).then_inc(ot_copied, 1)

            def attention():
                split_at(S_KV, 0, 2, 1, KD)
                rms("dn0")
                split_at(S_KV, 1, 2, 0, KD)
                for k in range(KD):
                    run(xq_hi[:, k, :], h[:, k, :], ACT.Copy, scale=gain(G_ATT)[:, k:k + 1]).then_inc(xq_hi_done, 1)
                split_at(S_KV, 1, 2, 1, KD)
                split_at(S_Q, 0, 2, 0, KD)
                act.wait_ge(v_full, 1)
                run(vtok[:, 0:4, :].rearrange("p n (a c) -> p a n c", a=2),
                    slot[2][:, :, :].rearrange("p a (n c) -> p a n c", n=4), ACT.Copy).then_inc(v_copied, 1)
                run(vtok[0:META, 4, :], slot[3][0:META, 0, 0:2 * P], ACT.Copy).then_inc(v_copied, 1)
                split_at(S_Q, 0, 2, 1, KD)

                def heads(j, hp, par, ahead):
                    for t in range(GRP):
                        three = slice(GRP * t, GRP * (t + 1))
                        act.wait_ge(m_ready, hp * GRP + (t + 1))
                        for n in range(GRP * t, GRP * (t + 1)):
                            if n == GRP * t + 1:
                                run(esnk[:, par, three], mneg[:, par, three], ACT.Exp, bias=column(sink, hp))
                            ins = run(prob[:, par, n, :], prob[:, par, n, :], ACT.Exp, bias=mneg[:, par, n:n + 1],
                                      accum_out=den[:, par, n:n + 1])
                        ins.then_inc(exp_done, 1)
                    if ahead:
                        split_at(S_Q, j, 2, 2 + par, KD)
                    act.wait_ge(pv_done, hp + 1)
                    run(tile_of(ao_hi, hp, META, L), slot[2][:, 1, :], ACT.Copy)
                    run(tile_of(ao_hi, hp, 0, META), slot[3][:, 0, 0:META], ACT.Copy).then_inc(ao_hi_done, 1)

                heads(0, 0, 0, True)
                heads(0, 1, 1, True)
                with act.Fori(1, KVH - 1) as j:
                    for e in range(2):
                        heads(j, act.snap(j * 2 + e), e, True)
                heads(KVH - 1, HP - 2, 0, True)
                heads(KVH - 1, HP - 1, 1, False)

                def o_tile(m, par):
                    if isinstance(m, int):
                        split(S_O + m + 1, 1 - par, landed(1 - par, S_O + m + 1), KD)
                    else:
                        split(m + (S_O + 1), 1 - par, m * 8 + landed(1 - par, S_O + 1), KD)
                    if not (isinstance(m, int) and m == 0):
                        residual("o", m - 1 if isinstance(m, int) else act.snap(m - 1), 1 - par, G_FFN[1])

                o_tile(0, 0)
                o_tile(1, 1)
                with act.Fori(1, KD // 2) as i:
                    for e in range(2):
                        o_tile(act.snap(i * 2 + e), e)
                residual("o", KD - 1, 1, G_FFN[1])

            act.wait_ge(slab_used, S_UP0)
            for k in range(KD):
                run(xa_hi[:, k, :], h[:, k, :], ACT.Copy, scale=gain(G_FFN[0])[:, k:k + 1]
                    ).then_inc(x_hi_done["glu"], 1)
            up("up0", 0, S_UP0, "glu", KS)
            down("dn0", S_DN0, G_KV, KD)
            attention()
            up("up1", 1, S_UP1, "o", KS)
            down("dn1", S_DN1, None, 0)
            act.wait_ge(fin_full, 1)
            run(rinv[:, 0:4], slot[3][:, 1, 0:4], ACT.Sqrt, scale=1.0 / D, bias=eps[:, :]).then_inc(fin_rms, 1)
            act.wait_ge(fin_rinv, 1)
            for n in (0, 2):
                run(otok[:, n, :], otok[:, n, :], ACT.Copy, scale=rinv[:, n:n + 1]).then_inc(scaled_act, 1)

        @block.tensor
        def _(pe):
            mm, tr = nc.tensor.matmul, nc.tensor.transpose

            def begin(name):
                n = fill_of[name]
                if n >= 4:
                    pe.wait_ge(s5_free[n % 4], n // 4)
                return slot[n % 4]

            pe.wait_ge(consts_set, 1)
            pe.wait_ge(par_ready, 1)
            pe.wait_ge(g5_in, 16 * T)
            pe.wait_ge(rows_in, 16 * 7)
            ps = begin("par")
            for n, name in enumerate(("lbr", "lbi", "cr", "ci")):
                tr(ps[:, 0, n * PAIRS:(n + 1) * PAIRS], pm[name][0:PAIRS, :], ident[0:PAIRS, 0:PAIRS])
            tr(ps[:, 0, 128:128 + G], g5row[0:G, :], ident[0:G, 0:G])
            tr(ps[:, 0, 192:192 + 5 * KD], grow[0:5 * KD, :], ident[0:5 * KD, 0:5 * KD])
            for n in range(3):
                ins = tr(ps[:, 0, 232 + n * 4 * KF:232 + (n + 1) * 4 * KF], crow[0:4 * KF, n * P:(n + 1) * P],
                         ident[0:4 * KF, 0:4 * KF])
            ins.then_inc(s5_full, 1)
            pe.wait_ge(c_in, 64)
            for r in range(2):
                ps = begin(f"c{r}")
                for k in range(KD):
                    ins = tr(ps[:, k // 4, (k % 4) * P:(k % 4 + 1) * P],
                             craw[r][:, k].rearrange("p t s -> p (t s)"), ident[:, :])
                ins.then_inc(s5_full, 1)
            pe.wait_ge(xn_ready, T)
            for b in range(8):
                ps = begin(f"u{b}")
                for n in range(8):
                    ins = tr(ps[:, n // 4, (n % 4) * NC:(n % 4 + 1) * NC], xn[0:NC, 8 * b + n].rearrange("c t h -> c (t h)"),
                             ident[0:NC, 0:NC])
                ins.then_inc(s5_full, 1)
            for b in range(8):
                pe.wait_ge(win_t_ready, b + 1)
                ps = begin(f"w{b}")
                for r in range(2):
                    for q in range(4):
                        ins = tr(ps[:, r, q * P:(q + 1) * P],
                                 win_t[:, b % 2, r, q].rearrange("p t h -> p (t h)"), ident[:, :])
                ins.then_inc(s5_full, 1)
                copied_wait(pe, f"w{b}")
                if b == 0:
                    for n in range(8):
                        copied_wait(pe, f"u{n}")
                ps = begin(f"v{b}")
                for q in range(4):
                    for r in range(2):
                        for t in range(2):
                            col = ((q % 2) * 2 + r) * (NC - 1)
                            ins = mm(ps[t * S:(t + 1) * S, q // 2, col:col + NC - 1],
                                     win[:, b % 2, r, q, t * S:(t + 1) * S],
                                     u5[:, 2 * (4 * b + q) + t, 0:NC - 1], start=True, stop=True)
                ins.then_inc(s5_full, 1)
            copied_wait(pe, "c0")
            copied_wait(pe, "c1")
            pe.wait_ge(bpad_ready, 1)
            for b in range(4):
                pe.wait_ge(cpow_ready, 2 * b + 2)
                ps = begin(f"g{b}")
                for n in range(8):
                    q = 8 * b + n
                    for r in range(2):
                        ins = mm(ps[0:2 * HC, n // 4, (n % 4) * TH:(n % 4 + 1) * TH],
                                 bpad[r][:, q].rearrange("p g h -> p (g h)"),
                                 cpow[r][:, q, 0:T, :].rearrange("p k h -> p (k h)"), start=r == 0, stop=r == 1)
                ins.then_inc(s5_full, 1)
            pe.wait_ge(xt_in, 32)
            for k in range(KD):
                ps = begin(f"h{k}")
                tr(ps[:, 0, 0:META], xt[0:META, 4 * D + k * P:4 * D + (k + 1) * P], ident[0:META, 0:META])
                for n in range(4):
                    col = (META, META + P, 0, P)[n]
                    ins = tr(ps[:, n // 2, col:col + P], xt[:, n * D + k * P:n * D + (k + 1) * P], ident[:, :])
                ins.then_inc(s5_full, 1)

            def outputs(k):
                pe.wait_ge(toep_in[k // 2], 32 * T)
                ps = begin(f"y{k}")
                for n in range(8):
                    g, u = 8 * k + n, 2 * k + n // 4
                    if n % 4 == 0:
                        pe.wait_ge(zpad_ready, u + 1)
                    o = ps[0:NC, n // 4, (n % 4) * TH:(n % 4 + 1) * TH]
                    mm(o, u5[:, g, :], toep[:, g, :], start=True, stop=False)
                    for r in range(2):
                        ins = mm(o, zpad[:, u % 3, (n // 2) % 2, n % 2, r, :],
                                 cpow[r][:, g // 2, 1:T + 1, :].rearrange("p k h -> p (k h)"),
                                 start=False, stop=r == 1)
                    if n == 3:
                        ins.then_inc(zpad_used, 1)
                ins.then_inc(s5_full, 1)

            def operand(k):
                copied_wait(pe, f"y{k}")
                ps = begin(f"t{k}")
                for t in range(T):
                    ins = tr(ps[:, t // 4, (t % 4) * NC:(t % 4 + 1) * NC], gy[0:NC, k % 2, t, :], ident[0:NC, 0:NC])
                ins.then_inc(s5_full, 1)

            pe.wait_ge(scan_done, NC - 1)
            outputs(0)
            for k in range(1, KD):
                outputs(k)
                operand(k - 1)
            operand(KD - 1)

            def slab(s, buf, dst, x_hi, x_lo, k0=0, nk=KD, opens=True, closes=True, ready=None, cut=HALF):
                pe.wait_ge(hi_done, s + 1)
                pe.wait_ge(lo_done, s + 1)
                for k in range(nk):
                    if ready is not None:
                        ready(k)
                    for n, (w, xx) in enumerate(((w_hi, x_hi), (w_hi, x_lo), (w_lo, x_hi))):
                        for half, (a, b) in enumerate(((0, cut), (cut, L))):
                            ins = mm(slot[dst][:, half, 0:b - a], w[:, buf, k * P:(k + 1) * P], xx[:, k0 + k, a:b],
                                     start=opens and k == 0 and n == 0, stop=closes and k == nk - 1 and n == 2)
                ins.then_inc(slab_used, 1)

            def operand_ready(p):
                def ready(k):
                    pe.wait_ge(x_hi_done[p], k + 1)
                    pe.wait_ge(x_lo_done[p], k + 1)
                return ready

            def statistics(p):
                pe.wait_ge(acc_done[p], KD)
                for half in range(2):
                    ins = mm(slot[3][:, half, 0:HALF], ones[:, :], acc[:, half * HALF:(half + 1) * HALF],
                             start=True, stop=True)
                ins.then_inc(stat_full[p], 1)

            def glu_ready(k):
                pe.wait_ge(glu_x_hi, k + 1)
                copied_wait(pe, f"t{k}")

            def glu_pair(m, e):
                for q in range(2):
                    if isinstance(m, int) and m < 2:
                        pe.wait_ge(s5_free[2 * e + q], N_FILLS[2 * e + q])
                    elif q == 0:
                        pe.wait_ge(glu_mul, m - 1)
                    slab(m * 2 + (S_GLU + q), q, 2 * e + q, xa_hi, xa_lo,
                         ready=glu_ready if isinstance(m, int) and m == 0 and q == 0 else None)

            glu_pair(0, 0)
            glu_pair(1, 1)
            with pe.Fori(1, KD // 2) as i:
                for e in range(2):
                    glu_pair(pe.snap(i * 2 + e), e)

            def up(p, base, before, slots_free):
                for q in range(4):
                    slots_free(q)
                    if q == 3:
                        pe.wait_ge(stat_read[before], 1)
                    slab(base + q, q % 2, q, xa_hi, xa_lo, ready=operand_ready(before) if q == 0 else None)
                    if q == 0:
                        slots_free(3)
                        statistics(before)
                with pe.Fori(1, KF // 2) as i:
                    for q in range(4):
                        pe.wait_ge(up_evicted[p], i * 4 + (q - 3))
                        slab(i * 4 + (base + q), q % 2, q, xa_hi, xa_lo)

            def down(p, base, before, hook=None):
                def tile(m, e):
                    if isinstance(m, int) and m < 2:
                        pe.wait_ge(up_evicted[before], 2 * KF - 3 + e)
                    else:
                        pe.wait_ge(h_done[p], m - 1)
                    if isinstance(m, int) and m == 0:
                        pe.wait_ge(act_hi_done[before], KF - 1)
                        pe.wait_ge(act_lo_done[before], KF - 1)
                    slab(m * 2 + base, 0, e, act_hi, act_lo, 0, KS, True, False)
                    if isinstance(m, int) and m == 0:
                        pe.wait_ge(act_hi_done[before], KF)
                        pe.wait_ge(act_lo_done[before], KF)
                    slab(m * 2 + (base + 1), 1, e, act_hi, act_lo, KS, KS, False, True)
                    if hook is not None:
                        hook(m, e)

                tile(0, 0)
                tile(1, 1)
                with pe.Fori(1, KD // 2) as i:
                    for e in range(2):
                        tile(pe.snap(i * 2 + e), e)

            def attention():
                for q in range(4):
                    if q < 2:
                        pe.wait_ge(h_done["dn0"], KD - 1 + q)
                    if q == 3:
                        pe.wait_ge(stat_read["dn0"], 1)
                    slab(S_KV + q, q % 2, q, xa_hi, xa_lo, ready=operand_ready("dn0") if q == 0 else None)
                    if q == 0:
                        statistics("dn0")

                def q_slab(hp, e, first=False):
                    def ready(k):
                        pe.wait_ge(xq_hi_done, k + 1)
                        pe.wait_ge(xq_lo_done, k + 1)
                    if first:
                        pe.wait_ge(kv_evicted, 1)
                    else:
                        pe.wait_ge(q_evicted, hp)
                    slab(hp + S_Q, e, 0, xq_hi, xq_lo, ready=ready if first else None, cut=Q_CUT)

                q_slab(0, 0, True)
                pe.wait_ge(kv_evicted, 4)
                for a in range(2):
                    for n in range(4):
                        tr(slot[2][:, a, n * P:(n + 1) * P], kvt[:, 2 + a, META + n * P:META + (n + 1) * P],
                           ident[:, :])
                    ins = tr(slot[3][0:META, 0, a * P:(a + 1) * P], kvt[:, 2 + a, 0:META], ident[:, :])
                ins.then_inc(v_full, 1)
                pe.wait_ge(v_copied, 2)

                bank = [slot[1][:, 0, :], slot[1][:, 1, :], slot[2][:, 0, :]]
                o_real, o_meta = slot[2][:, 1, :], slot[3][:, 0, :]

                def heads(j, hp, e, ahead):
                    peeled = isinstance(hp, int)
                    for t in range(GRP):
                        for n in range(GRP):
                            ins = mm(bank[t][:, n * KEYS:(n + 1) * KEYS],
                                     qt[:, e, GRP * t + n].rearrange("p x f -> p (x f)"), kcur[:, GRP * t + n, :],
                                     start=True, stop=True)
                        ins.then_inc(scores_done, 1)
                    if ahead:
                        q_slab(hp + 1, 1 - e)

                    def transposes(t):
                        pe.wait_ge(p_ready, hp * GRP + (t + 1))
                        for n in range(GRP):
                            tr(bank[t][:, n * P:(n + 1) * P], prob[:, e, GRP * t + n, 0:BAND], ident[:, :])
                        tr(bank[t][0:GRP * META, GRP * P:(GRP + 1) * P], probm[:, e, GRP * t:GRP * (t + 1), :].rearrange("p n j -> p (n j)"),
                           ident[:, :]).then_inc(pt_full, 1)

                    def product(t):
                        pe.wait_ge(pt_copied, hp * GRP + (t + 1))
                        for n in range(GRP):
                            blk = GRP * t + n
                            for half in range(2):
                                part = slice(half * HD, (half + 1) * HD)
                                o = o_real[part, blk * CH:(blk + 1) * CH] if blk < NCH else o_meta[part, 0:CH]
                                if blk < NCH:
                                    mm(o, vcur[:, blk, :], pt[:, blk, part], start=True, stop=False)
                                ins = mm(o, vmet[:, n, :], ptm[:, t, part],
                                         start=blk == NCH, stop=True)
                        return ins

                    transposes(0)
                    transposes(1)
                    if not peeled or hp >= 1:
                        pe.wait_ge(ao_lo_done, hp)
                    pe.wait_ge(v_in, j * 80 + 80)
                    product(0)
                    transposes(2)
                    product(1)
                    if ahead:
                        pe.wait_ge(q_evicted, hp + 2)
                        if e == 1:
                            pe.wait_ge(k_in, j * 96 + 192)
                    product(2).then_inc(pv_done, 1)

                pe.wait_ge(q_evicted, 1)
                pe.wait_ge(k_in, 96)
                heads(0, 0, 0, True)
                heads(0, 1, 1, True)
                with pe.Fori(1, KVH - 1) as j:
                    for e in range(2):
                        heads(j, pe.snap(j * 2 + e), e, True)
                heads(KVH - 1, HP - 2, 0, True)
                heads(KVH - 1, HP - 1, 1, False)

                def o_tile(m, e):
                    if isinstance(m, int) and m == 0:
                        pe.wait_ge(q_evicted, HP)
                        pe.wait_ge(ao_hi_done, HP)
                        pe.wait_ge(ao_lo_done, HP)
                    elif isinstance(m, int) and m == 1:
                        pe.wait_ge(pt_copied, GRP * HP)
                    else:
                        pe.wait_ge(h_done["o"], m - 1)
                    slab(m + S_O, e, e, ao_hi, ao_lo)

                o_tile(0, 0)
                o_tile(1, 1)
                with pe.Fori(1, KD // 2) as i:
                    for e in range(2):
                        o_tile(pe.snap(i * 2 + e), e)

            up("up0", S_UP0, "glu", lambda q: pe.wait_ge(glu_mul, KD - 1 + q // 2))
            down("dn0", S_DN0, "up0")
            attention()
            up("up1", S_UP1, "o", lambda q: pe.wait_ge(h_done["o"], KD - 1 + min(q, 1)))
            def out_tile(m, e):
                pe.wait_ge(hg_done, m + 1)
                if isinstance(m, int) and m < 2:
                    pe.wait_ge(up_evicted["up1"], 2 * KF - 1 + m)
                else:
                    pe.wait_ge(ot_copied, m - 1)
                for n in range(4):
                    ins = tr(slot[2 + e][:, 0, n * P:(n + 1) * P], sig[:, e, META + n * P:META + (n + 1) * P],
                             ident[:, :])
                ins.then_inc(ot_full, 1)

            def hook(m, e):
                if isinstance(m, int):
                    if m >= 1:
                        out_tile(m - 1, 1 - e)
                else:
                    out_tile(pe.snap(m - 1), 1 - e)

            down("dn1", S_DN1, "up1", hook)
            out_tile(KD - 1, 1)
            pe.wait_ge(acc_done["dn1"], KD)
            for n in range(4):
                ins = mm(slot[3][:, 1, n:n + 1], acc[:, META + n * P:META + (n + 1) * P], ones[:, 0:1],
                         start=True, stop=True)
            ins.then_inc(fin_full, 1)

        @block.vector
        def _(dve):
            chain = Chain(dve, dve_chain)
            tt, ts, stt = nc.vector.tensor_tensor, nc.vector.tensor_scalar, nc.vector.scalar_tensor_tensor
            copy = nc.vector.tensor_copy
            link = chain.link
            LN2_HI, LN2_LO = 0.693359375, -2.12194440e-4
            PI2_A, PI2_B = 6.28125, 0.00193500518798828125
            PI2_C = float(2 * np.pi - PI2_A - PI2_B)
            PI_IN = 3.1415925

            def exp_small(o, v, n, f, q, whole):
                link(ts(v, v, -87.0, 88.0, ALU.max, ALU.min))
                link(ts(n, v, float(1 / np.log(2.0)), MAGIC, ALU.mult, ALU.add))
                link(ts(n, n, MAGIC, None, ALU.subtract))
                link(stt(f, n, -LN2_HI, v, ALU.mult, ALU.add))
                link(stt(f, n, -LN2_LO, f, ALU.mult, ALU.add))
                link(ts(q, f, 1.0 / 5040, None, ALU.mult))
                for c in (1.0 / 720, 1.0 / 120, 1.0 / 24, 1.0 / 6, 0.5, 1.0):
                    link(stt(q, q, c, f, ALU.add, ALU.mult))
                link(ts(n, n, 127.0, None, ALU.add))
                link(copy(whole, n))
                link(ts(whole, whole, 23, None, ALU.logical_shift_left))
                link(stt(o, q, 1.0, whole.bitcast(F32), ALU.add, ALU.mult))

            def cmul(o, a, b, tmp):
                tt(o[0], a[0], b[0], ALU.mult)
                tt(tmp[0], a[1], b[1], ALU.mult)
                tt(o[1], a[0], b[1], ALU.mult)
                chain.did(tt(tmp[1], a[1], b[0], ALU.mult))
                chain.sync()
                tt(o[0], o[0], tmp[0], ALU.subtract)
                chain.did(tt(o[1], o[1], tmp[1], ALU.add))
                chain.sync()

            for hp in range(HP):
                for half in range(2):
                    nc.vector.memset(negslope[half * CH:(half + 1) * CH, hp:hp + 1],
                                     -float(2.0 ** (-8.0 * (2 * hp + half + 1) / HEADS)))

            for r in range(2):
                nc.vector.memset(bpad[r], 0.0)

            dve.wait_ge(par_in, 48)
            a = {n: t[0:PAIRS, :] for n, t in pm.items()}
            pair = lambda t: t.rearrange("p (t s) -> p t s", t=2)
            exp_small(stp[0:PAIRS, :], lst[0:PAIRS, :], se["a"][0:PAIRS, :], se["b"][0:PAIRS, :], se["c"][0:PAIRS, :],
                      sei[0:PAIRS, :])
            step = stp[0:PAIRS, :, None].to_broadcast([PAIRS, 2, S])
            link(ts(a["lr"], a["lr"], -1e-4, None, ALU.min))
            tt(pair(a["ar"]), pair(a["lr"]), step, ALU.mult)
            link(tt(pair(a["th"]), pair(a["li"]), step, ALU.mult))
            link(ts(a["n"], a["th"], float(1 / (2 * np.pi)), MAGIC, ALU.mult, ALU.add))
            link(ts(a["n"], a["n"], MAGIC, None, ALU.subtract))
            link(stt(a["a"], a["n"], -PI2_A, a["th"], ALU.mult, ALU.add))
            link(stt(a["a"], a["n"], -PI2_B, a["a"], ALU.mult, ALU.add))
            link(stt(a["a"], a["n"], -PI2_C, a["a"], ALU.mult, ALU.add))
            link(ts(a["b"], a["a"], float(np.pi / 2), None, ALU.add))
            link(ts(a["d"], a["b"], float(np.pi), -float(2 * np.pi), ALU.is_gt, ALU.mult))
            link(tt(a["b"], a["b"], a["d"], ALU.add))
            ts(a["b"], a["b"], -PI_IN, PI_IN, ALU.max, ALU.min)
            ts(a["a"], a["a"], -PI_IN, PI_IN, ALU.max, ALU.min).then_inc(angles_ready, 1)
            exp_small(a["r"], a["ar"], a["n"], a["cr"], a["ci"], pi[0:PAIRS, :])
            dve.wait_ge(sincos_ready, 1)
            tt(a["lbr"], a["r"], a["c"], ALU.mult)
            tt(a["lbi"], a["r"], a["s"], ALU.mult)
            tt(a["d"], a["lr"], a["lr"], ALU.mult)
            link(tt(a["th"], a["li"], a["li"], ALU.mult))
            ts(a["n"], a["lbr"], 1.0, None, ALU.subtract)
            link(tt(a["d"], a["d"], a["th"], ALU.add))
            nc.vector.reciprocal(a["d"], a["d"])
            tt(a["cr"], a["n"], a["lr"], ALU.mult)
            tt(a["a"], a["lbi"], a["li"], ALU.mult)
            tt(a["ci"], a["lbi"], a["lr"], ALU.mult)
            link(tt(a["b"], a["n"], a["li"], ALU.mult))
            tt(a["cr"], a["cr"], a["a"], ALU.add)
            link(tt(a["ci"], a["ci"], a["b"], ALU.subtract))
            tt(a["cr"], a["cr"], a["d"], ALU.mult)
            tt(a["ci"], a["ci"], a["d"], ALU.mult).then_inc(par_ready, 1)
            dve.wait_ge(ssq5_ready, 1)
            nc.vector.reciprocal(rst5[0:NC, :], ssq5[0:NC, :]).then_inc(rst5_ready, 1)
            full_wait(dve, "par")
            ps = fslot("par")
            for r in range(2):
                copy(lpow[r][:, 1, :], ps[:, 0, r * PAIRS:(r + 1) * PAIRS])
                copy(coef[r][:, :], ps[:, 0, (2 + r) * PAIRS:(3 + r) * PAIRS])
                nc.vector.memset(lpow[r][:, 0, :], 1.0 - r)
            copy(gain5[:, :], ps[:, 0, 128:128 + G])
            copy(gains[:, :], ps[:, 0, 192:192 + 5 * KD])
            for half in range(2):
                part = slice(half * CH, (half + 1) * CH)
                copy(sink[part, :], sinkrow[part, :].rearrange("p (a b) -> p a b", b=2)[:, :, half])
            last = copy(conv_w[:, :], ps[:, 0, 232:232 + 12 * KF])
            frees(last, "par")
            copied_wait(dve, "par")
            for n in (1, 2, 4):
                tmp = [dtmp[r][:, 0:n * PAIRS].rearrange("p (k q) -> p k q", k=n) for r in range(2)]
                cmul([lpow[r][:, n + 1:2 * n + 1, :] for r in range(2)], [lpow[r][:, 1:n + 1, :] for r in range(2)],
                     [lpow[r][:, n:n + 1, :].to_broadcast([P, n, PAIRS]) for r in range(2)], tmp)
            nc.vector.memset(zst[:, :, :, 0], 0.0)
            for r in range(2):
                copy(l8a[:, :, r], lpow[0][:, T, :])
                ins = ts(l8b[:, :, r], lpow[1][:, T, :], (-1.0, 1.0)[r], None, ALU.mult)
            ins.then_inc(lpow_ready, 1)
            dve.wait_ge(b_in, 32)
            cmul([bbar[r][:, :, :] for r in range(2)],
                 [coef[r][:, :, None].to_broadcast([P, PAIRS, HC]) for r in range(2)], braw,
                 [dtmp[r][:, :].rearrange("p (q h) -> p q h", q=PAIRS) for r in range(2)])

            for r in range(2):
                for g2 in range(2):
                    part = slice(g2 * S, (g2 + 1) * S)
                    ins = copy(bpad[r][part, :, g2, :], bbar[r][part, :, :])
            ins.then_inc(bpad_ready, 1)

            def in_map(b):
                if b >= 2:
                    full_wait(dve, f"w{b - 2}")
                lp = [lpow[r][:, T - 1::-1, 4 * b:4 * b + 4].rearrange("p t q -> p q t")[:, :, :, None]
                      .to_broadcast([P, 4, T, HC]) for r in range(2)]
                bb = [bbar[r][:, 4 * b:4 * b + 4, None, :].to_broadcast([P, 4, T, HC]) for r in range(2)]
                tmp = [dtmp[r][:, :].rearrange("p (q t h) -> p q t h", q=4, t=T) for r in range(2)]
                o = [win_t[:, b % 2, r] for r in range(2)]
                tt(o[0], lp[0], bb[0], ALU.mult)
                tt(tmp[0], lp[1], bb[1], ALU.mult)
                tt(o[1], lp[0], bb[1], ALU.mult)
                link(tt(tmp[1], lp[1], bb[0], ALU.mult))
                tt(o[0], o[0], tmp[0], ALU.subtract)
                tt(o[1], o[1], tmp[1], ALU.add).then_inc(win_t_ready, 1)
                dve.wait_ge(win_t_ready, b + 1)

            dve.wait_ge(xn_ready, T)
            in_map(0)
            in_map(1)
            for b in range(8):
                full_wait(dve, f"u{b}")
                g8 = slice(8 * b, 8 * b + 8)
                frees(tt(u5[:, g8, :].rearrange("p (a g) c -> p a g c", a=2),
                         fslot(f"u{b}")[:, :, 0:4 * NC].rearrange("p a (g c) -> p a g c", g=4),
                         gain5[:, g8].rearrange("p (a g) -> p a g", a=2)[:, :, :, None].to_broadcast([P, 2, 4, NC]),
                         ALU.mult), f"u{b}")
            for b in range(8):
                full_wait(dve, f"v{b}")
                frees(copy(zst[:, 4 * b:4 * b + 4, :, 1:NC].rearrange("p (a q) r c -> p a (q r) c", a=2),
                           fslot(f"v{b}")[:, :, 0:4 * (NC - 1)].rearrange("p a (x c) -> p a x c", x=4)), f"v{b}")
                if b + 2 < 8:
                    in_map(b + 2)
            copied_wait(dve, "v7")
            chain.sync()

            for c in range(NC - 1):
                cur, nxt = zst[:, :, :, c], zst[:, :, :, c + 1]
                tt(st1, l8a, cur, ALU.mult)
                link(tt(st2, l8b, cur[:, :, 1::-1], ALU.mult))
                link(tt(st1, st1, st2, ALU.add))
                tt(nxt, nxt, st1, ALU.add).then_inc(scan_done, 1)
                dve.wait_ge(scan_done, c + 1)

            def pad_states(u):
                if u >= 3:
                    if (u - 3) % 2 == 0:
                        dve.wait_ge(zpad_used, (u - 3) // 2 + 1)
                    else:
                        full_wait(dve, f"y{(u - 3) // 2}")
                for g2 in range(2):
                    part = slice(g2 * S, (g2 + 1) * S)
                    ins = copy(zpad[part, u % 3, :, g2], zst[part, 2 * u:2 * u + 2])
                ins.then_inc(zpad_ready, 1)

            def glu_x_low(k):
                name = f"t{k}"
                dve.wait_ge(glu_x_hi, k + 1)
                for half in range(2):
                    view = lambda t: t[:, k, :].rearrange("p (c b t) -> p b t c", b=2, t=T // 2)[:, half]
                    ins = tt(view(xa_lo), fslot(name)[:, half, 0:4 * NC].rearrange("p (t c) -> p t c", t=4),
                             f32(view(xa_hi)), ALU.subtract)
                frees(ins, name)

            dve.wait_ge(zpad_zero, 1)
            for u in range(3):
                pad_states(u)
            for k in range(KD):
                for u in (2 * k + 3, 2 * k + 4):
                    if u < 2 * KD:
                        pad_states(u)
                if k >= 1:
                    glu_x_low(k - 1)
            glu_x_low(KD - 1)

            def update(p, m, e, g, last_slab):
                dve.wait_ge(slab_used, last_slab)
                hm = halves(tile_of(h, m))
                tt(hm, acc_of(e), hm, ALU.add).then_inc(h_done[p], 1)
                if g is not None:
                    dve.wait_ge(x_hi_done[p], m + 1)
                    stt(tile_of(xa_lo, m), tile_of(h, m), column(gain(g), m), f32(tile_of(xa_hi, m)),
                        ALU.mult, ALU.subtract).then_inc(x_lo_done[p], 1)

            def inverse_rms(p, scaled=False):
                dve.wait_ge(stat_read[p], 1)
                nc.vector.reciprocal(rinv[:, :], rinv[:, :]).then_inc(rinv_ready[p], 1)
                dve.wait_ge(rinv_ready[p], 1)
                if scaled:
                    ts(rinv8[:, :], rinv[:, :], HD ** -0.5, None, ALU.mult).then_inc(rinv_ready[p], 1)

            def loop_2(n, body):
                body(0, 0)
                body(1, 1)
                k0 = chain.k
                with dve.Fori(1, n // 2) as i:
                    for e in range(2):
                        body(dve.snap(i * 2 + e), e)
                assert chain.k == k0, "the chain does not count here"

            def glu(m, e):
                dve.wait_ge(glu_sig, m + 1)
                tt(halves(sig[:, e, :]), acc_of(2 * e), halves(sig[:, e, :]), ALU.mult).then_inc(glu_mul, 1)
                dve.wait_ge(glu_mul, m + 1)
                tt(tile_of(h, m), tile_of(h, m), sig[:, e, :], ALU.add).then_inc(h_done["glu"], 1)

            for k in range(KD):
                copied_wait(dve, f"h{k}")
            loop_2(KD, glu)

            def up(p, l, before):
                inverse_rms(before)
                per = 3

                def tile(m):
                    w = lambda q, t: column(cw[:, l, t, :], m if q == 0 else (m + KF if isinstance(m, int)
                                                                              else dve.snap(m + KF)))
                    first = isinstance(m, int) and m == 0
                    for q in range(2):
                        dve.wait_ge(slab_used, m * 2 + ((S_UP0, S_UP1)[l] + q + 1))
                        tt(halves(ubuf[:, q, 2:L + 2]), acc_of_q(q, m), halves(rinv[:, :]), ALU.mult
                           ).then_inc(up_evicted[p], 1)
                        dve.wait_ge(tap_done[p], m * 2 + (q + 1))
                        link(stt(cbuf[:, q, :], ubuf[:, q, 1:L + 1], w(q, 1), cbuf[:, q, :], ALU.mult, ALU.add))
                        ins = stt(cbuf[:, q, :], ubuf[:, q, 0:L], w(q, 0), cbuf[:, q, :], ALU.mult, ALU.add)
                        if q == 0:
                            ins.then_inc(conv_gate[p], 1)
                        else:
                            link(ins)
                    dve.wait_ge(silu_done[p], m + 1)
                    if not first:
                        dve.wait_ge(act_hi_done[p], m)
                        dve.wait_ge(act_lo_done[p], m)
                    tt(abuf[:, :], cbuf[:, 0, :], cbuf[:, 1, :], ALU.mult).then_inc(act_done[p], 1)

                par = [0]

                def acc_of_q(q, m):
                    return acc_of(2 * par[0] + q)

                dve.wait_ge(ubuf_zero, l + 1)
                for m in range(2):
                    par[0] = m
                    tile(m)
                with dve.Fori(1, KF // 2) as i:
                    chain.loop(i, 2 * per)
                    for e in range(2):
                        par[0] = e
                        tile(dve.snap(i * 2 + e))
                chain.leave(KF // 2 - 1, 2 * per)

            def attention():
                inverse_rms("dn0", scaled=True)
                dve.wait_ge(rinv_ready["dn0"], 2)
                for q in range(4):
                    dve.wait_ge(slab_used, S_KV + q + 1)
                    tt(halves(kvt[:, q, :]), acc_of(q), halves(rinv[:, :]), ALU.mult).then_inc(kv_evicted, 1)
                    for k in range(2 * q, 2 * q + 2):
                        dve.wait_ge(xq_hi_done, k + 1)
                        stt(xq_lo[:, k, :], h[:, k, :], gain(G_ATT)[:, k:k + 1], f32(xq_hi[:, k, :]),
                            ALU.mult, ALU.subtract).then_inc(xq_lo_done, 1)
                dve.wait_ge(dist_set, 1)
                bank = [slot[1][:, 0, :], slot[1][:, 1, :], slot[2][:, 0, :]]

                def q_out(hp, e):
                    dve.wait_ge(slab_used, hp + (S_Q + 1))
                    if not isinstance(hp, int) or hp >= 2:
                        dve.wait_ge(scores_done, (hp - 1) * GRP)
                    for x in range(2):
                        part = slice(x * HD, (x + 1) * HD)
                        real = slot[0][part].rearrange("p a n -> p (a n)")[:, META:META + 2 * (512 - META)].rearrange(
                            "p (a n) -> p a n", a=2)[:, :, 0:SEQ // 2]
                        tt(qt[part, e, 0:NCH, x, :].rearrange("p (a n) f -> p a n f", a=2),
                           real.rearrange("p a (n f) -> p a n f", f=CH),
                           rinv8[part, META:L].rearrange("p (a n f) -> p a n f", a=2, f=CH), ALU.mult)
                        ins = tt(qt[part, e, NCH, x, 0:META], slot[0][part, 0, 0:META], rinv8[part, 0:META], ALU.mult)
                    ins.then_inc(q_evicted, 1)

                def heads(hp, e, ahead):
                    def scores(t):
                        three = slice(GRP * t, GRP * (t + 1))
                        dve.wait_ge(scores_done, hp * GRP + (t + 1))
                        s = prob[:, e, three, :]
                        link(stt(s, dist[:, three, :], column(negslope, hp),
                                 bank[t][:, 0:GRP * KEYS].rearrange("p (n j) -> p n j", n=GRP), ALU.mult, ALU.add))
                        link(nc.vector.reduce_max(mneg[:, e, three], s, AX.X))
                        ts(mneg[:, e, three], mneg[:, e, three], column(sink, hp), -1.0, ALU.max, ALU.mult
                           ).then_inc(m_ready, 1)

                    def denominators(t):
                        three = slice(GRP * t, GRP * (t + 1))
                        dve.wait_ge(exp_done, hp * GRP + (t + 1))
                        link(tt(rden[:, e, three], den[:, e, three], esnk[:, e, three], ALU.add))
                        nc.vector.reciprocal(rden[:, e, three], rden[:, e, three]).then_inc(rden_ready, 1)

                    scores(0)
                    scores(1)
                    denominators(0)
                    scores(2)
                    denominators(1)
                    denominators(2)
                    if ahead:
                        q_out(hp + 1 if isinstance(hp, int) else dve.snap(hp + 1), 1 - e)
                    for t in range(GRP):
                        three = slice(GRP * t, GRP * (t + 1))
                        dve.wait_ge(pt_full, hp * GRP + (t + 1))
                        if t == 0 and (not isinstance(hp, int) or hp >= 1):
                            dve.wait_ge(pv_done, hp)
                        copy(pt[:, three, :], bank[t][:, 0:GRP * P].rearrange("p (n q) -> p n q", n=GRP))
                        copy(ptm[0:GRP * META, t, :], bank[t][0:GRP * META, GRP * P:(GRP + 1) * P]
                             ).then_inc(pt_copied, 1)
                    dve.wait_ge(ao_hi_done, hp + 1)
                    tt(tile_of(ao_lo, hp, META, L), slot[2][:, 1, :], f32(tile_of(ao_hi, hp, META, L)), ALU.subtract)
                    tt(tile_of(ao_lo, hp, 0, META), slot[3][:, 0, 0:META], f32(tile_of(ao_hi, hp, 0, META)), ALU.subtract
                       ).then_inc(ao_lo_done, 1)

                dve.wait_ge(pads_zero, 1)
                q_out(0, 0)
                heads(0, 0, True)
                heads(1, 1, True)
                per = 2 * (GRP * 3)
                with dve.Fori(1, KVH - 1) as j:
                    chain.loop(j, per)
                    for e in range(2):
                        heads(dve.snap(j * 2 + e), e, True)
                chain.leave(KVH - 2, per)
                heads(HP - 2, 0, True)
                heads(HP - 1, 1, False)
                loop_2(KD, lambda m, e: update("o", m, e, G_FFN[1], m + (S_O + 1)))

            for k in range(KD):
                dve.wait_ge(x_hi_done["glu"], k + 1)
                stt(xa_lo[:, k, :], h[:, k, :], gain(G_FFN[0])[:, k:k + 1], f32(xa_hi[:, k, :]),
                    ALU.mult, ALU.subtract).then_inc(x_lo_done["glu"], 1)
            up("up0", 0, "glu")
            loop_2(KD, lambda m, e: update("dn0", m, e, G_KV, m * 2 + (S_DN0 + 2)))
            attention()
            up("up1", 1, "o")
            def out_update(m, e):
                update("dn1", m, e, None, m * 2 + (S_DN1 + 2))
                dve.wait_ge(h_done["dn1"], m + 1)
                if not isinstance(m, int) or m >= 2:
                    dve.wait_ge(ot_full, m - 1)
                ts(sig[:, e, :], tile_of(h, m), column(gain(G_FIN), m), None, ALU.mult).then_inc(hg_done, 1)

            loop_2(KD, out_update)
            dve.wait_ge(fin_rms, 1)
            nc.vector.reciprocal(rinv[:, 0:4], rinv[:, 0:4]).then_inc(fin_rinv, 1)
            dve.wait_ge(fin_rinv, 1)
            dve.wait_ge(ot_copied, KD)
            for n in (1, 3):
                ts(otok[:, n, :], otok[:, n, :], rinv[:, n:n + 1], None, ALU.mult).then_inc(scaled_dve, 1)

        @block.gpsimd
        def _(pool):
            chain = Chain(pool, pool_chain)
            link = chain.link
            tt, ts, memset = nc.gpsimd.tensor_tensor, nc.gpsimd.tensor_scalar, nc.gpsimd.memset

            link(memset(ident[:, :], 0.0))
            nc.gpsimd.affine_select(out=ident[:, :], in_=ident[:, :], compare_op=ALU.not_equal, fill=1.0, base=0,
                                    pattern=[[-1, P]], channel_multiplier=1)
            memset(ones[:, :], 1.0)
            memset(eps[:, :], EPS).then_inc(consts_set, 1)
            pool.wait_ge(d_in, 32)
            pool.wait_ge(consts_set, 1)
            link(tt(diag2[0:2 * HC, :], ident[0:2 * HC, 0:HC], ident[0:2 * HC, HC:2 * HC], ALU.add))
            tt(dskip[0:2 * HC], drow[0:2 * HC], diag2[0:2 * HC, None, :].to_broadcast([2 * HC, PAIRS, HC]), ALU.mult
               ).then_inc(dskip_ready, 1)
            pool.wait_ge(lpow_ready, 1)
            copied_wait(pool, "c0")
            copied_wait(pool, "c1")
            for b in range(8):
                q4 = slice(4 * b, 4 * b + 4)
                c0 = [cpow[r][:, q4, 0, None, :].to_broadcast([P, 4, T, HC]) for r in range(2)]
                lp = [lpow[r][:, 1:T + 1, q4].rearrange("p k q -> p q k")[:, :, :, None].to_broadcast([P, 4, T, HC])
                      for r in range(2)]
                o = [cpow[r][:, q4, 1:T + 1, :] for r in range(2)]
                tmp = ptmp[:, 0:4 * T * HC].rearrange("p (q k h) -> p q k h", q=4, k=T)
                tt(o[0], c0[0], lp[0], ALU.mult)
                link(tt(tmp, c0[1], lp[1], ALU.mult))
                tt(o[1], c0[1], lp[0], ALU.mult)
                link(tt(o[0], o[0], tmp, ALU.add))
                link(tt(tmp, c0[0], lp[1], ALU.mult))
                tt(o[1], o[1], tmp, ALU.subtract).then_inc(cpow_ready, 1)
                pool.wait_ge(cpow_ready, b + 1)
            for b in range(8):
                copied_wait(pool, f"u{b}")
            memset(toep[:, :, :], 0.0).then_inc(toep_zero, 1)
            pool.wait_ge(win_t_ready, 8)
            memset(zpad, 0.0).then_inc(zpad_zero, 1)
            pool.wait_ge(dskip_ready, 1)
            for b in range(4):
                copied_wait(pool, f"g{b}")
                kd = kern[0:2 * HC, b % 2, :, 0:HC]
                tt(kd, kd, dskip[0:2 * HC, 8 * b:8 * (b + 1), :], ALU.add).then_inc(kern_d_ready, 1)

            def low(s, buf, nk):
                pool.wait_ge(hi_done, s + 1)
                tt(w_lo[:, buf, 0:nk * P], raw[:, buf, 0:nk * P], f32(w_hi[:, buf, 0:nk * P]), ALU.subtract
                   ).then_inc(lo_done, 1)

            def add_square(p, m, par):
                pool.wait_ge(sq_done[p], m + 1)
                if isinstance(m, int) and m == 0:
                    pool.wait_ge(acc_zero[p], 1)
                else:
                    pool.wait_ge(acc_done[p], m)
                tt(acc[:, :], acc[:, :], sq[:, par, :], ALU.add).then_inc(acc_done[p], 1)

            def loop_2(n, body):
                body(0, 0, False)
                body(1, 1, False)
                if n > 4:
                    with pool.Fori(1, n // 2 - 1) as i:
                        for e in range(2):
                            body(pool.snap(i * 2 + e), e, False)
                body(n - 2, 0, False)
                body(n - 1, 1, True)

            less = lambda m: m - 1 if isinstance(m, int) else pool.snap(m - 1)
            is0 = lambda m: isinstance(m, int) and m == 0

            low(0, 0, KD)

            def glu(m, e, last):
                low(m * 2 + (S_GLU + 1), 1, KD)
                if is0(m):
                    for name in ("y6", "y7"):
                        copied_wait(pool, name)
                    pool.wait_ge(s5_full, len(fills))
                    memset(acc[:, :], 0.0).then_inc(acc_zero["glu"], 1)
                    memset(vcur[0:CH, 0, :], 0.0)
                    memset(ubuf[:, :, 0:2], 0.0).then_inc(ubuf_zero, 1)
                else:
                    add_square("glu", less(m), 1 - e)
                low(m * 2 + (S_GLU + 2), 0, KD)

            loop_2(KD, glu)
            add_square("glu", KD - 1, 1)

            def up(p, base, before):
                def act_low(m):
                    pool.wait_ge(act_hi_done[p], m + 1)
                    tt(tile_of(act_lo, m), abuf[:, :], f32(tile_of(act_hi, m)), ALU.subtract).then_inc(act_lo_done[p], 1)

                def tile(m, e, last):
                    low(m * 2 + (base + 1), 1, KD)
                    if not is0(m):
                        act_low(less(m))
                    low(m * 2 + (base + 2), 0, KS if last else KD)

                loop_2(KF, tile)
                act_low(KF - 1)

            def down(p, base, nxt):
                def tile(m, e, last):
                    if is0(m):
                        pool.wait_ge(act_done[{"dn0": "up0", "dn1": "up1"}[p]], KF)
                        if p == "dn0":
                            pool.wait_ge(stat_full["glu"], 1)
                            d = dint[:, :].rearrange("p (n j) -> p n j", n=NQ)
                            for half in range(2):
                                part = slice(half * CH, (half + 1) * CH)
                                io = nc.gpsimd.iota
                                io(d[part, 0:NCH, 0:BAND], pattern=[[0, NCH], [-1, BAND]], base=CH, channel_multiplier=1)
                                io(d[part, 0:NCH, BAND:KEYS], pattern=[[CH, NCH], [-1, META]], base=META,
                                   channel_multiplier=1)
                                io(d[part, NCH, 0:BAND], pattern=[[-1, BAND]], base=0, channel_multiplier=1)
                                io(d[part, NCH, BAND:KEYS], pattern=[[-1, META]], base=0, channel_multiplier=1
                                   ).then_inc(dint_set, 1)
                                pool.wait_ge(dint_set, half + 1)
                        pool.wait_ge(stat_full[{"dn0": "glu", "dn1": "o"}[p]], 1)
                        memset(acc[:, :], 0.0).then_inc(acc_zero[p], 1)
                    low(m * 2 + (base + 1), 1, KS)
                    if not is0(m):
                        add_square(p, less(m), 1 - e)
                    if not last or nxt:
                        low(m * 2 + (base + 2), 0, nxt if last else KS)

                loop_2(KD, tile)
                add_square(p, KD - 1, 1)

            def attention():
                low(S_KV + 1, 1, KD)
                low(S_KV + 2, 0, KD)
                pool.wait_ge(dist_abs, 1)
                memset(dist[:, 0, 0:CH], FAR)
                memset(dist[:, NCH, 0:BAND], FAR).then_inc(dist_set, 1)
                low(S_KV + 3, 1, KD)
                low(S_Q, 0, KD)
                pool.wait_ge(slab_used, S_Q)
                memset(kcur[:, 0, 0:CH], 0.0)
                memset(kcur[:, NCH, 0:BAND], 0.0)
                memset(qt, 0.0)
                memset(ptm, 0.0)
                memset(vmet, 0.0).then_inc(pads_zero, 1)
                low(S_Q + 1, 1, KD)

                def heads(j, hp, e, ahead):
                    for t in range(GRP):
                        three = slice(GRP * t, GRP * (t + 1))
                        pool.wait_ge(rden_ready, hp * GRP + (t + 1))
                        s = prob[:, e, three, :]
                        tt(s[:, :, 0:BAND], s[:, :, 0:BAND], rden[:, e, three, None].to_broadcast([P, GRP, BAND]), ALU.mult)
                        tt(probm[:, e, three, :], s[:, :, BAND:KEYS], rden[:, e, three, None].to_broadcast([P, GRP, META]),
                           ALU.mult).then_inc(p_ready, 1)
                    if ahead:
                        low(hp + (S_Q + 2), e, KD)

                heads(0, 0, 0, True)
                heads(0, 1, 1, True)
                with pool.Fori(1, KVH - 1) as j:
                    for e in range(2):
                        heads(j, pool.snap(j * 2 + e), e, True)
                heads(KVH - 1, HP - 2, 0, True)
                heads(KVH - 1, HP - 1, 1, False)
                pool.wait_ge(stat_full["dn0"], 1)
                memset(acc[:, :], 0.0).then_inc(acc_zero["o"], 1)
                pool.wait_ge(ao_lo_done, HP)
                memset(ubuf[:, :, 0:2], 0.0).then_inc(ubuf_zero, 1)

                def o_tile(m, e, last):
                    low(m + (S_O + 1), 1 - e, KD)
                    if not is0(m):
                        add_square("o", less(m), 1 - e)

                loop_2(KD, o_tile)
                add_square("o", KD - 1, 1)

            up("up0", S_UP0, "glu")
            down("dn0", S_DN0, KD)
            attention()
            up("up1", S_UP1, "o")
            down("dn1", S_DN1, 0)


_INS = ['x', 'meta', 's5_norm', 's5_lambda_re', 's5_lambda_im', 's5_log_step', 's5_b_re', 's5_b_im', 's5_c_re',
        's5_c_im', 's5_d', 's5_w_glu', 'kv_norm', 'w_kv', 'attn_norm', 'w_q', 'sinks', 'w_o', 'ffn_norm', 'ffn_w_up',
        'ffn_conv', 'ffn_w_down', 'final_norm']


def kernel(**inputs):
    import concourse.bacc as bacc
    from concourse.bass_utils import run_bass_kernel_spmd

    nc = bacc.Bacc("TRN2", target_bir_lowering=False, num_devices=1)
    arrays, args = {}, []
    for name in _INS:
        a = np.ascontiguousarray(inputs[name])
        arrays[f"in_{name}"] = a
        args.append(nc.dram_tensor(f"in_{name}", a.shape, mybir.dt.from_np(a.dtype), kind="ExternalInput").ap())
    out = nc.dram_tensor("out", (1, SEQ, D), F32, kind="ExternalOutput").ap()
    k_scratch = nc.dram_tensor("k_scratch", (KVH, HD, L), F32, kind="Internal").ap()
    v_scratch = nc.dram_tensor("v_scratch", (L, KVH * HD), F32, kind="Internal").ap()
    trunk(nc, *args, out, k_scratch, v_scratch)
    r = run_bass_kernel_spmd(nc, [arrays], core_ids=[0])
    return r.results[0]["out"]
```

```python
from contextlib import ExitStack

import numpy as np

import concourse.bass as bass
from concourse import mybir

F32 = mybir.dt.float32
F32R = mybir.dt.float32r
I32 = mybir.dt.int32
ACT = mybir.ActivationFunctionType
ALU = mybir.AluOpType
AX = mybir.AxisListType

P = 128
D = 1024
SEQ = 512
META = 16
L = SEQ + META
HALF = L // 2
KD = D // P
FFN = 2816
KF = FFN // P
EPS = 1e-6
G, S, HC = 64, 64, 16
T = 8
NC = L // T
PAIRS = G // 2
POOL_MAPS = 7
NV = NC - 1
TH = T * HC
CH = 64
NCH = SEQ // CH
NQ = NCH + 1
BAND = 2 * CH
KEYS = BAND + META
HD = 64
HEADS = 16
KVH = 4
HP = HEADS // 2
CONV = 3
LIVE = (META - (CONV - 1)) // 4 * 4
MID = META + SEQ // 2
ALL_TOKENS = ((0, HALF), (HALF, L))
LIVE_TOKENS = ((LIVE, (LIVE + L) // 2), ((LIVE + L) // 2, L))
Q_LEAD = META - LIVE
Q_TOKENS = ((LIVE, MID), (MID - Q_LEAD, L))
REAL_TOKENS = ((META, MID), (MID, L))
Q_PART = 7
GRP = 3
FAR = 1e30
MAGIC = 1.5 * 2.0 ** 23

S_GLU = 0
S_UP0 = S_GLU + 2 * KD
S_DN0 = S_UP0 + 2 * KF
S_KV = S_DN0 + 2 * KD
S_Q = S_KV + 4
S_O = S_Q + KD
S_UP1 = S_O + KD
S_DN1 = S_UP1 + 2 * KF
S_END = S_DN1 + 2 * KD
KS = KF // 2


class Chain:

    def __init__(self, eng, sem):
        self.eng, self.sem, self.base, self.moving, self.k = eng, sem, 0, None, 0

    def did(self, ins):
        self.k += 1
        ins.then_inc(self.sem, 1)
        return self.value()

    def value(self):
        v = self.base + self.k
        return v if self.moving is None else self.moving + v

    def wait(self, value):
        self.eng.wait_ge(self.sem, value)

    def sync(self):
        self.eng.wait_ge(self.sem, self.value())

    def link(self, ins):
        self.did(ins)
        self.sync()

    def loop(self, i, per):
        self.base, self.k = self.base + self.k - per, 0
        self.moving = self.eng.snap(i * per)

    def leave(self, n, per):
        assert self.k == per, (self.k, per)
        self.base, self.k, self.moving = self.base + per * (n + 1), 0, None


def trunk(nc, x, meta, s5_norm, s5_lambda_re, s5_lambda_im, s5_log_step, s5_b_re, s5_b_im, s5_c_re, s5_c_im,
          s5_d, s5_w_glu, kv_norm, w_kv, attn_norm, w_q, sinks, w_o, ffn_norm, ffn_w_up, ffn_conv, ffn_w_down,
          final_norm, out, k_scratch, v_scratch):

    first = (nc.sbuf_base + 31) // 32 * 8
    last = nc.sbuf_usable_end // 4

    def at(name, col, cols, dtype=F32):
        assert first + col + cols <= last, name
        return nc.alloc_sbuf_tensor_at(name, [P, cols], dtype, offset=4 * (first + col))

    class Zone:

        def __init__(self, col, cols):
            self.col, self.end = col, col + cols

        def put(self, name, cols, dtype=F32):
            assert self.col + cols <= self.end, (name, self.col + cols - self.end)
            t = at(name, self.col, cols, dtype)
            self.col += (cols + 7) // 8 * 8
            return t

    W_RAW, W_SPL = 2 * KS * P, 4 * KS * P
    Z_K = 0
    Z_H = Z_K + 616
    Z_RAW = Z_H + KD * L
    Z_SPL = Z_RAW + W_RAW
    Z_A = Z_SPL + W_SPL
    Z_B = Z_A + 2 * KD * L
    Z_C = Z_B + 2 * KF * L
    C_COLS = last - first - Z_C

    z = Zone(Z_K, Z_H - Z_K)
    ident = z.put("ident", P)
    ones = z.put("ones", P)
    gains = z.put("gains", 5 * KD)
    conv_w = z.put("conv_w", 2 * 3 * 2 * KF)
    negslope = z.put("negslope", HP)
    sink = z.put("sink", HP)
    eps = z.put("eps", 1)
    gain = lambda g: gains[:, g * KD:(g + 1) * KD]
    G_FFN = [0, 3]
    G_KV, G_ATT, G_FIN = 1, 2, 4
    cw = conv_w[:].rearrange("p (l t m) -> p l t m", l=2, t=3)

    h = at("h", Z_H, KD * L)[:].rearrange("p (k n) -> p k n", k=KD)
    raw = at("raw", Z_RAW, W_RAW)[:].rearrange("p (b c) -> p b c", b=2)
    zs = Zone(Z_SPL, W_SPL)
    w_hi = zs.put("w_hi", W_SPL // 2, F32R)[:].rearrange("p (b c) -> p b c", b=2)
    w_lo = zs.put("w_lo", W_SPL // 2, F32R)[:].rearrange("p (b c) -> p b c", b=2)
    tiles = lambda t, n: t[:].rearrange("p (k n) -> p k n", k=n)
    za = Zone(Z_A, 2 * KD * L)
    xa_hi = tiles(za.put("xa_hi", KD * L, F32R), KD)
    xa_lo = tiles(za.put("xa_lo", KD * L, F32R), KD)
    zb = Zone(Z_B, 2 * KF * L)
    act_hi = tiles(zb.put("act_hi", KF * L, F32R), KF)
    act_lo = tiles(zb.put("act_lo", KF * L, F32R), KF)
    f32 = lambda ap: ap.bitcast(F32)

    def tile_of(t, m, a=0, b=L):
        return t[:, m, a:b] if isinstance(m, int) else t[:, bass.ds(m, 1), a:b].rearrange("p a n -> p (a n)")

    def column(t, m):
        return t[:, m:m + 1] if isinstance(m, int) else t[:, bass.ds(m, 1)]

    za = Zone(Z_A, 2 * KD * L)
    xc = za.put("xc", T * D)
    za = Zone(Z_A, 2 * KD * L)
    zb = Zone(Z_B, 2 * KF * L)
    u5 = zb.put("u5", G * NC)[:].rearrange("p (g c) -> p g c", g=G)
    cpow = [zb.put(f"cpow{r}", PAIRS * (T + 1) * HC)[:].rearrange("p (q k h) -> p q k h", q=PAIRS, k=T + 1)
            for r in range(2)]
    toep = zb.put("toep", G * TH)[:].rearrange("p (g c) -> p g c", g=G)
    xn = at("xn", Z_B + G * NC + 2 * PAIRS * (T + 1) * HC, G * TH)[:].rearrange(
        "p (g t h) -> p g t h", g=G, t=T)
    zpad = zb.put("zpad", 3 * 8 * NC)[:].rearrange("p (u q g r c) -> p u q g r c", u=3, q=2, g=2, r=2)
    Z_ZPAD = zb.col - 3 * 8 * NC
    ltmp = [at(f"ltmp{n}", Z_ZPAD + 512 * n, 512) for n in range(2)]
    xt = at("xt", Z_B + G * NC + 2 * PAIRS * (T + 1) * HC, 4 * D)
    xt_meta = at("xt_meta", Z_B + G * NC + PAIRS * (T + 1) * HC, D)
    dtmp = [at(f"dtmp{n}", Z_A + 14 * L + 520 * n, 520) for n in range(2)]
    zc = Zone(Z_C, C_COLS)
    phase = zc.put("phase", PAIRS * 2 * NV)[:].rearrange("p (q r c) -> p q r c", q=PAIRS, r=2)
    zrot = zc.put("zrot", 2 * 8 * NV)[:].rearrange("p (b q r c) -> p b q r c", b=2, q=4, r=2)
    gy = zc.put("gy", 2 * T * P)[:].rearrange("p (b t c) -> p b t c", b=2, t=T)
    lpow = [zc.put(f"lpow{r}", PAIRS * (T + 1))[:].rearrange("p (k q) -> p k q", k=T + 1) for r in range(2)]
    coef = [zc.put(f"coef{r}", PAIRS) for r in range(2)]
    rho = zc.put("rho", PAIRS)
    ph = [zc.put(f"ph{n}", 2 * PAIRS)[:].rearrange("p (r q) -> p r q", r=2) for n in range(2)]
    gain5 = zc.put("gain5", G)
    ssq5 = zc.put("ssq5", T)
    rst5 = zc.put("rst5", T)
    zp = Zone(Z_C, 2 * PAIRS * NC)
    pm = {n: zp.put("pm_" + n, P) for n in ("lr", "li", "ar", "ai", "r", "th", "n", "s", "c", "a", "b", "d",
                                            "lbr", "lbi", "cr", "ci")}
    pi = zp.put("pm_int", P, I32)
    lst = zp.put("lst", 2)
    stp = zp.put("stp", 2)
    se = {n: zp.put("se_" + n, 2) for n in ("a", "b", "c", "d")}
    sei = zp.put("se_int", 2, I32)
    g5row = zp.put("g5row", TH)
    grow = zp.put("grow", P)
    crow = zp.put("crow", 3 * P)
    sinkrow = zp.put("sinkrow", HEADS)
    zh = Zone(Z_H, KD * L)
    win_t = zh.put("win_t", 2 * 2 * 4 * TH)[:].rearrange("p (b r q t h) -> p b r q t h", b=2, r=2, q=4, t=T)
    win = zh.put("win", 2 * 2 * 4 * P)[:].rearrange("p (b r q s) -> p b r q s", b=2, r=2, q=4)
    zr = Zone(Z_RAW, W_RAW)
    bbar = [zr.put(f"bbar{r}", PAIRS * HC)[:].rearrange("p (q h) -> p q h", q=PAIRS) for r in range(2)]
    dskip = zr.put("dskip", PAIRS * HC)[:].rearrange("p (q h) -> p q h", q=PAIRS)
    drow = zr.put("drow", PAIRS * HC)[:].rearrange("p (q h) -> p q h", q=PAIRS)
    diag2 = zr.put("diag2", HC)
    ptmp = zr.put("ptmp", 4 * T * HC)
    zs = Zone(Z_SPL, W_SPL)
    braw = [zs.put(f"braw{r}", PAIRS * HC)[:].rearrange("p (q h) -> p q h", q=PAIRS) for r in range(2)]
    craw = [zs.put(f"craw{r}", KD * 2 * S)[:].rearrange("p (r t s) -> p r t s", r=KD, t=2) for r in range(2)]
    zs = Zone(Z_SPL, W_SPL)
    kern = zs.put("kern", 2 * 8 * TH)[:].rearrange("p (b q c) -> p b q c", b=2, q=8)
    zs = Zone(Z_SPL + 4 * TH * 7, W_SPL - 4 * TH * 7)
    bpad = [zs.put(f"bpad{r}", PAIRS * 2 * HC)[:].rearrange("p (q g h) -> p q g h", q=PAIRS, g=2) for r in range(2)]

    zc = Zone(Z_C, C_COLS)
    rinv = zc.put("rinv", L)
    rinv8 = zc.put("rinv8", L)
    acc = zc.put("acc", L)
    sq = tiles(zc.put("sq", 2 * L), 2)
    ubuf = tiles(zc.put("ubuf", 2 * (L + 2)), 2)
    cbuf = tiles(zc.put("cbuf", 2 * L), 2)
    abuf = zc.put("abuf", L)
    sig = tiles(zc.put("sig", 2 * L), 2)
    dist = zc.put("dist", NQ * KEYS)[:].rearrange("p (n j) -> p n j", n=NQ)
    vcur = zc.put("vcur", NCH * HD)[:].rearrange("p (n d) -> p n d", n=NCH)
    zc = Zone(Z_C + 3 * L + 2 * L, 2 * (L + 2) + 2 * L + L)
    mneg = tiles(zc.put("mneg", 2 * NQ), 2)
    den = tiles(zc.put("den", 2 * NQ), 2)
    esnk = tiles(zc.put("esnk", 2 * NQ), 2)
    rden = tiles(zc.put("rden", 2 * NQ), 2)
    dint = zc.put("dint", KEYS * NQ, I32)
    zb = Zone(Z_B, 2 * KF * L)
    xq_hi = tiles(zb.put("xq_hi", KD * L, F32R), KD)
    xq_lo = tiles(zb.put("xq_lo", KD * L, F32R), KD)
    ao_hi = tiles(zb.put("ao_hi", KD * L, F32R), KD)
    ao_lo = tiles(zb.put("ao_lo", KD * L, F32R), KD)
    kvt = tiles(zb.put("kvt", 4 * L), 4)
    vtok = zb.put("vtok", 5 * 2 * P)[:].rearrange("p (n c) -> p n c", n=5)
    za = Zone(Z_A, 2 * KD * L)
    qt = za.put("qt", 2 * NQ * P)[:].rearrange("p (e n x f) -> p e n x f", e=2, n=NQ, x=2)
    kcur = za.put("kcur", NQ * KEYS)[:].rearrange("p (n j) -> p n j", n=NQ)
    prob = za.put("prob", 2 * NQ * KEYS)[:].rearrange("p (b n j) -> p b n j", b=2, n=NQ)
    probm = za.put("probm", 2 * NQ * META)[:].rearrange("p (b n j) -> p b n j", b=2, n=NQ)
    pt = za.put("pt", NQ * P)[:].rearrange("p (n q) -> p n q", n=NQ)
    ptm = za.put("ptm", GRP * P)[:].rearrange("p (t q) -> p t q", t=GRP)
    vmet = za.put("vmet", GRP * HD)[:].rearrange("p (n d) -> p n d", n=GRP)
    za = Zone(Z_A, 2 * KD * L)
    otok = za.put("otok", 4 * D)[:].rearrange("p (n c) -> p n c", n=4)

    up_v = [ffn_w_up[l].rearrange("(k p) c -> p k c", p=P) for l in range(2)]
    dn_v = [ffn_w_down[l].rearrange("(k p) c -> p k c", p=P) for l in range(2)]
    glu_v = s5_w_glu[0].rearrange("(k p) c -> p k c", p=P)
    kv_v = w_kv.rearrange("(k p) c -> p k c", p=P)
    q_v = w_q[0].rearrange("(k p) c -> p k c", p=P)
    o_v = w_o[0].rearrange("(k p) c -> p k c", p=P)

    ctx = ExitStack()
    with ctx:
        sem = lambda name: ctx.enter_context(nc.semaphore(name))
        slot = [ctx.enter_context(nc.psum_tensor(f"slot{n}", [P, 2, 512], F32)) for n in range(4)]
        acc_of = lambda n: slot[n][:, :, 0:HALF]
        halves = lambda ap: ap.rearrange("p (a n) -> p a n", a=2)
        live_of = lambda n: slot[n][:, :, 0:(L - LIVE) // 2]
        real_of = lambda n: slot[n][:, :, 0:SEQ // 2]

        raw_landed = [sem("raw_landed0"), sem("raw_landed1")]
        hi_done, lo_done, slab_used = sem("hi_done"), sem("lo_done"), sem("slab_used")
        act_chain, dve_chain, pool_chain = sem("act_chain"), sem("dve_chain"), sem("pool_chain")

        consts_set, x_in, par_in, rows_in, b_in, c_in, g5_in, d_in, xt_in = (
            sem(n) for n in ("consts_set", "x_in", "par_in", "rows_in", "b_in", "c_in", "g5_in", "d_in", "xt_in"))
        angles_ready, sincos_ready, par_ready, ssq5_ready, rst5_ready, xn_ready = (
            sem(n) for n in ("angles_ready", "sincos_ready", "par_ready", "ssq5_ready", "rst5_ready", "xn_ready"))
        s5_full = sem("s5_full")
        s5_free = [sem(f"s5_free{n}") for n in range(4)]
        lpow_ready, cpow_ready, dskip_ready, toep_zero = (
            sem(n) for n in ("lpow_ready", "cpow_ready", "dskip_ready", "toep_zero"))
        win_t_ready, kern_d_ready = (sem(n) for n in ("win_t_ready", "kern_d_ready"))
        phase_1 = sem("phase_1")
        bpad_zero, bpad_ready, zpad_zero, zpad_ready, zpad_used = (
            sem(n) for n in ("bpad_zero", "bpad_ready", "zpad_zero", "zpad_ready", "zpad_used"))
        toep_in = [sem(f"toep_in{b}") for b in range(4)]
        glu_x_hi = sem("glu_x_hi")
        glu_sig, glu_mul, ubuf_zero = sem("glu_sig"), sem("glu_mul"), sem("ubuf_zero")
        RES = ("glu", "dn0", "o", "dn1")
        h_done, sq_done, acc_zero, acc_done, x_hi_done, x_lo_done = (
            {p: sem(f"{n}_{p}") for p in RES} for n in ("h_done", "sq_done", "acc_zero", "acc_done", "x_hi_done",
                                                        "x_lo_done"))
        stat_full, stat_read, rinv_ready = (
            {p: sem(f"{n}_{p}") for p in ("glu", "dn0", "o")} for n in ("stat_full", "stat_read", "rinv_ready"))
        UPS = ("up0", "up1")
        up_evicted, tap_done, conv_gate, silu_done, act_done, act_hi_done, act_lo_done = (
            {p: sem(f"{n}_{p}") for p in UPS} for n in ("up_evicted", "tap_done", "conv_gate", "silu_done", "act_done",
                                                        "act_hi_done", "act_lo_done"))
        dint_set, dist_abs, dist_set, pads_zero = (sem(n) for n in ("dint_set", "dist_abs", "dist_set", "pads_zero"))
        kv_evicted, v_full, v_copied, k_written, v_written, k_in, v_in = (
            sem(n) for n in ("kv_evicted", "v_full", "v_copied", "k_written", "v_written", "k_in", "v_in"))
        xq_hi_done, xq_lo_done, q_evicted, scores_done, m_ready, exp_done, rden_ready, p_ready = (
            sem(n) for n in ("xq_hi_done", "xq_lo_done", "q_evicted", "scores_done", "m_ready", "exp_done",
                             "rden_ready", "p_ready"))
        pt_full, pt_copied, pv_done, ao_hi_done, ao_lo_done = (
            sem(n) for n in ("pt_full", "pt_copied", "pv_done", "ao_hi_done", "ao_lo_done"))
        hg_done, ot_full, ot_copied, fin_full, fin_rms, fin_rinv, scaled_act, scaled_dve, written = (
            sem(n) for n in ("hg_done", "ot_full", "ot_copied", "fin_full", "fin_rms", "fin_rinv", "scaled_act",
                             "scaled_dve", "written"))

        block = ctx.enter_context(nc.Block())

        fills = ["par", "c0", "c1"] + [f"u{b}" for b in range(8)]
        for b in range(8):
            fills += [f"w{b}", f"v{b}"] + [f"g{b // 2}"] * (b % 2 == 0)
            fills += [f"y{b - 2}"] * (b >= 2) + [f"t{b - 3}"] * (b >= 3)
        fills += ["y6", "t5", "y7", "t6", "h0", "h1", "h2", "h3", "t7", "h4", "h5", "h6", "h7"]
        fill_of = {name: n for n, name in enumerate(fills)}
        fslot = lambda name: slot[fill_of[name] % 4]
        N_FILLS = [len([n for n in range(len(fills)) if n % 4 == k]) for k in range(4)]

        def full_wait(eng, name):
            eng.wait_ge(s5_full, fill_of[name] + 1)

        def copied_wait(eng, name):
            n = fill_of[name]
            eng.wait_ge(s5_free[n % 4], n // 4 + 1)

        def frees(ins, name):
            ins.then_inc(s5_free[fill_of[name] % 4], 1)

        @block.sync
        def _(sp):
            dma = sp.dma_start
            dma(pm["lr"][0:PAIRS, :], s5_lambda_re[0].rearrange("(q t) s -> q (t s)", t=2)).then_inc(par_in, 16)
            dma(pm["li"][0:PAIRS, :], s5_lambda_im[0].rearrange("(q t) s -> q (t s)", t=2)).then_inc(par_in, 16)
            dma(lst[0:PAIRS, :], s5_log_step[0].rearrange("(q t) -> q t", t=2)).then_inc(par_in, 16)
            dma(xc[0:2, :], meta.rearrange("(c t) d -> c (t d)", t=T)).then_inc(x_in, 16)
            dma(xc[2:NC, :], x[0].rearrange("(c t) d -> c (t d)", t=T)).then_inc(x_in, 16)
            for t in range(T):
                dma(g5row[0:G, t * HC:(t + 1) * HC], s5_norm[0].rearrange("(g h) -> g h", g=G)).then_inc(g5_in, 16)
            for n, g in enumerate((ffn_norm[0], kv_norm, attn_norm[0], ffn_norm[1], final_norm)):
                dma(grow[n * KD:(n + 1) * KD, :], g.rearrange("(k p) -> k p", p=P)).then_inc(rows_in, 16)
            dma(crow[0:4 * KF, :].rearrange("q (r p) -> q r p", r=3),
                ffn_conv.rearrange("l t (m p) -> (l t m) p", p=P).rearrange("(r q) p -> q r p", r=3)
                ).then_inc(rows_in, 16)
            dma(sinkrow[:, :], sinks[0].partition_broadcast(P)).then_inc(rows_in, 16)
            for r, b in enumerate((s5_b_re, s5_b_im)):
                dma(braw[r], b[0].rearrange("(q t) s h -> (t s) q h", t=2)).then_inc(b_in, 16)
            for r, c in enumerate((s5_c_re, s5_c_im)):
                for t in range(2):
                    dma(craw[r][:, :, t, :],
                        c[0].rearrange("g h s -> (g h) s").rearrange("(r q) s -> q r s", r=KD)).then_inc(c_in, 16)
            for g2 in range(2):
                dma(drow[g2 * HC:(g2 + 1) * HC],
                    s5_d[0].rearrange("(q g h) -> g q h", g=2, h=HC)[g2].partition_broadcast(HC)).then_inc(d_in, 16)
            sp.wait_ge(toep_zero, 1)
            for b in range(4):
                sp.wait_ge(kern_d_ready, b + 1)
                for t in range(T):
                    for g2 in range(2):
                        dma(toep[t * HC:(t + 1) * HC, 16 * b:16 * (b + 1), t * HC:TH].rearrange(
                                "p (q g) c -> p q g c", g=2)[:, :, g2],
                            kern[g2 * HC:(g2 + 1) * HC, b % 2, :, 0:TH - t * HC]).then_inc(toep_in[b], 16)

            def load(buf, src, nk, split):
                if split is not None:
                    sp.wait_ge(hi_done, split)
                    sp.wait_ge(lo_done, split)
                dma(raw[:, buf, 0:nk * P].rearrange("p (k c) -> p k c", k=nk), src).then_inc(raw_landed[buf], 16)

            sp.wait_ge(win_t_ready, 8)
            load(0, glu_v[:, :, 0:P], KD, None)
            load(1, glu_v[:, :, D:D + P], KD, None)
            full_wait(sp, "y3")
            dma(xt[:, :].rearrange("p (n d) -> p n d", n=4), x[0].rearrange("(n p) d -> p n d", p=P)
                ).then_inc(xt_in, 16)
            dma(xt_meta[0:META, :], meta).then_inc(xt_in, 16)
            load(0, glu_v[:, :, P:2 * P], KD, 1)
            load(1, glu_v[:, :, D + P:D + 2 * P], KD, 2)

            def two_streams(w, start, turns, other, base):
                with sp.Fori(start, turns) as i:
                    cols = [sp.snap(i * (2 * P) + c) for c in (0, other, P, other + P)]
                    split = [sp.snap(i * 4 + (base + n - 1)) for n in range(4)]
                    for n in range(4):
                        load(n % 2, w[:, :, bass.ds(cols[n], P)], KD, split[n])

            def down(w, base):
                with sp.Fori(0, KD) as i:
                    col = sp.snap(i * P)
                    split = [sp.snap(i * 2 + (base + n - 1)) for n in range(2)]
                    for n in range(2):
                        load(n, w[:, n * KS:(n + 1) * KS, bass.ds(col, P)], KS, split[n])

            def one_stream(w, tiles, base):
                with sp.Fori(0, tiles // 2) as i:
                    cols = [sp.snap(i * (2 * P) + n * P) for n in range(2)]
                    split = [sp.snap(i * 2 + (base + n - 1)) for n in range(2)]
                    for n in range(2):
                        load(n, w[:, :, bass.ds(cols[n], P)], KD, split[n])

            two_streams(glu_v, 1, KD // 2, D, S_GLU)
            two_streams(up_v[0], 0, KF // 2, FFN, S_UP0)
            down(dn_v[0], S_DN0)
            one_stream(kv_v, 4, S_KV)
            for n in range(2):
                load(n, q_v[:, :, n * P:(n + 1) * P], KD, S_Q + n - 1)
            for a in range(2):
                sp.wait_ge(kv_evicted, a + 1)
                dma(k_scratch[2 * a:2 * a + 2].rearrange("t d n -> (t d) n"), kvt[:, a, :]).then_inc(k_written, 16)

            def k_load(j, scored):
                kj = k_scratch[bass.ds(j, 1)].rearrange("a d n -> (a d) n") if not isinstance(j, int) else k_scratch[j]
                if scored is not None:
                    sp.wait_ge(scores_done, scored)
                for half in range(2):
                    rows = slice(half * CH, (half + 1) * CH)
                    dma(kcur[rows, 1:NCH, 0:CH],
                        kj[:, META:L - CH].rearrange("d (n f) -> d n f", f=CH)).then_inc(k_in, 16)
                    dma(kcur[rows, 0:NCH, CH:BAND],
                        kj[:, META:L].rearrange("d (n f) -> d n f", f=CH)).then_inc(k_in, 16)
                    dma(kcur[rows, :, BAND:KEYS],
                        kj[:, None, 0:META].to_broadcast([HD, NQ, META])).then_inc(k_in, 16)

            def v_load(j64, used):
                if used is not None:
                    sp.wait_ge(pv_done, used)
                vj = v_scratch[:, bass.ds(j64, HD)]
                dma(vcur[0:CH, 1:NCH, :], vj[META:L - CH, :].rearrange("(n f) d -> f n d", f=CH)).then_inc(v_in, 16)
                dma(vcur[CH:P, 0:NCH, :], vj[META:L, :].rearrange("(n f) d -> f n d", f=CH)).then_inc(v_in, 16)
                for n in range(GRP):
                    dma(vmet[n * META:(n + 1) * META, n, :], vj[0:META, :]).then_inc(v_in, 16)

            sp.wait_ge(k_written, 32)
            sp.wait_ge(slab_used, S_Q)
            k_load(0, None)
            sp.wait_ge(v_copied, 2)
            dma(v_scratch[META:L, :].rearrange("(n p) c -> p n c", p=P), vtok[:, 0:4, :]).then_inc(v_written, 16)
            dma(v_scratch[0:META, :], vtok[0:META, 4, :]).then_inc(v_written, 16)
            sp.wait_ge(v_written, 32)
            sp.wait_ge(pads_zero, 1)
            v_load(0, None)
            with sp.Fori(1, KVH) as j:
                j64, scored, used = sp.snap(j * HD), sp.snap(j * (2 * GRP)), sp.snap(j * 2)
                jr = sp.snap(j * 1)
                cols = [sp.snap(j * (2 * P) + n * P) for n in range(2)]
                split = [sp.snap(j * 2 + (S_Q + n - 1)) for n in range(2)]
                for n in range(2):
                    load(n, q_v[:, :, bass.ds(cols[n], P)], KD, split[n])
                k_load(jr, scored)
                v_load(j64, used)
            one_stream(o_v, KD, S_O)
            two_streams(up_v[1], 0, KF // 2, FFN, S_UP1)
            down(dn_v[1], S_DN1)
            for n in range(4):
                sp.wait_ge((scaled_act, scaled_dve)[n % 2], n // 2 + 1)
                dma(out[0, n * P:(n + 1) * P, :], otok[:, n, :]).then_inc(written, 16)
            sp.wait_ge(written, 64)

        @block.scalar
        def _(act):
            chain = Chain(act, act_chain)
            run = nc.scalar.activation

            def split(s, buf, raw_count, nk):
                act.wait_ge(raw_landed[buf], raw_count)
                act.wait_ge(slab_used, s - 1)
                run(w_hi[:, buf, 0:nk * P], raw[:, buf, 0:nk * P], ACT.Copy).then_inc(hi_done, 1)

            def landed(buf, s):
                return 8 * (s - buf) + 16

            def split_at(base, m, per, q, nk):
                buf = (base + q) % 2
                split(m * per + (base + q), buf, m * (8 * per) + landed(buf, base + q), nk)

            act.wait_ge(angles_ready, 1)
            run(pm["s"][0:PAIRS, :], pm["a"][0:PAIRS, :], ACT.Sin)
            run(pm["c"][0:PAIRS, :], pm["b"][0:PAIRS, :], ACT.Sin).then_inc(sincos_ready, 1)
            act.wait_ge(x_in, 32)
            act.wait_ge(consts_set, 1)
            junk = win_t[0:NC].rearrange("p b r q t h -> p (b r q t h)")
            for t in range(T):
                if t >= 2:
                    chain.wait(chain.value() - 1)
                chain.did(run(junk[:, (t % 2) * D:(t % 2 + 1) * D], xc[0:NC, t * D:(t + 1) * D], ACT.Square,
                              accum_out=ssq5[0:NC, t:t + 1]))
            chain.sync()
            run(ssq5[0:NC, :], ssq5[0:NC, :], ACT.Sqrt, scale=1.0 / D, bias=eps[0:NC, :]).then_inc(ssq5_ready, 1)
            act.wait_ge(rst5_ready, 1)
            for t in range(T):
                run(xn[0:NC, :, t, :], xc[0:NC, t * D:(t + 1) * D].rearrange("c (g h) -> c g h", g=G), ACT.Copy,
                    scale=rst5[0:NC, t:t + 1]).then_inc(xn_ready, 1)
            for r in range(2):
                name = f"c{r}"
                full_wait(act, name)
                for t in range(2):
                    part = slice(t * S, (t + 1) * S)
                    ins = run(cpow[r][part, :, 0, :].rearrange("p (b x) h -> p b x h", b=2),
                              fslot(name)[part, :, :].rearrange("p b (x t h) -> p b x t h", t=2, h=HC)[:, :, :, t, :],
                              ACT.Copy, scale=(1.0, -1.0)[r])
                frees(ins, name)
            copied_wait(act, "par")
            for b in range(8):
                name = f"u{b}"
                full_wait(act, name)
                for n in range(8):
                    g = 8 * b + n
                    ins = run(u5[:, g, :], fslot(name)[:, n // 4, (n % 4) * NC:(n % 4 + 1) * NC], ACT.Copy,
                              scale=gain5[:, g:g + 1])
                frees(ins, name)

            def input_map(b):
                name = f"w{b}"
                full_wait(act, name)
                frees(run(win[:, b % 2].rearrange("p r q s -> p r (q s)"), fslot(name)[:, :, :], ACT.Copy), name)

            def kernels(b):
                name = f"g{b}"
                full_wait(act, name)
                if b >= 2:
                    act.wait_ge(toep_in[b - 2], 32 * T)
                frees(run(kern[0:2 * HC, b % 2].rearrange("p (a q) c -> p a (q c)", a=2), fslot(name)[0:2 * HC, :, :],
                          ACT.Copy), name)

            def gelu(k):
                name = f"y{k}"
                full_wait(act, name)
                if k >= 2:
                    full_wait(act, f"t{k - 2}")
                for half in range(2):
                    ins = run(gy[0:NC, k % 2].rearrange("c t (b g h) -> c b g t h", b=2, h=HC)[:, half],
                              fslot(name)[0:NC, half, :].rearrange("p (g t h) -> p g t h", g=4, t=T),
                              ACT.Gelu_apprx_tanh)
                frees(ins, name)

            def glu_operand(k):
                name = f"t{k}"
                full_wait(act, name)
                for half in range(2):
                    ins = run(xa_hi[:, k, :].rearrange("p (c b t) -> p b t c", b=2, t=T // 2)[:, half],
                              fslot(name)[:, half, 0:4 * NC].rearrange("p (t c) -> p t c", t=4), ACT.Copy)
                ins.then_inc(glu_x_hi, 1)

            def stream(k):
                name = f"h{k}"
                full_wait(act, name)
                run(h[:, k, 0:META + 2 * P], fslot(name)[:, 0, 0:META + 2 * P], ACT.Copy)
                frees(run(h[:, k, META + 2 * P:L], fslot(name)[:, 1, 0:2 * P], ACT.Copy), name)

            for b in range(8):
                input_map(b)
                if b % 2 == 0:
                    kernels(b // 2)
                if b >= 2:
                    gelu(b - 2)
                if b >= 3:
                    glu_operand(b - 3)
            gelu(6)
            glu_operand(5)
            gelu(7)
            glu_operand(6)
            for b in range(4):
                act.wait_ge(toep_in[b], 32 * T)
            act.wait_ge(raw_landed[0], 16)
            run(w_hi[:, 0, 0:KD * P], raw[:, 0, 0:KD * P], ACT.Copy).then_inc(hi_done, 1)
            for k in (0, 2):
                stream(k)
            glu_operand(7)
            for k in (4, 6):
                stream(k)

            def residual(p, m, par, g):
                act.wait_ge(h_done[p], m + 1)
                if not isinstance(m, int) or m >= 2:
                    act.wait_ge(acc_done[p], m - 1)
                run(sq[:, par, :], tile_of(h, m), ACT.Square).then_inc(sq_done[p], 1)
                if g is not None:
                    mi = m if isinstance(m, int) else act.snap(m)
                    run(tile_of(xa_hi, mi), tile_of(h, mi), ACT.Copy, scale=column(gain(g), mi)
                        ).then_inc(x_hi_done[p], 1)

            def rms(p):
                act.wait_ge(stat_full[p], 1)
                run(halves(rinv[:, :]), acc_of(3), ACT.Sqrt, scale=1.0 / D, bias=eps[:, :]).then_inc(stat_read[p], 1)

            def gate(m, par):
                act.wait_ge(slab_used, m * 2 + (S_GLU + 2))
                if not isinstance(m, int) or m >= 2:
                    act.wait_ge(h_done["glu"], m - 1)
                run(halves(sig[:, par, :]), acc_of(2 * par + 1), ACT.Sigmoid).then_inc(glu_sig, 1)

            def glu_tile(m, par, nxt=KD):
                if isinstance(m, int) and m == 0:
                    act.wait_ge(raw_landed[1], 16)
                    run(w_hi[:, 1, 0:KD * P], raw[:, 1, 0:KD * P], ACT.Copy).then_inc(hi_done, 1)
                else:
                    split_at(S_GLU, m, 2, 1, KD)
                    gate(m - 1, 1 - par)
                    residual("glu", m - 1, 1 - par, None)
                split_at(S_GLU, m, 2, 2, nxt)

            glu_tile(0, 0)
            glu_tile(1, 1)
            with act.Fori(1, KD // 2) as i:
                for e in range(2):
                    glu_tile(act.snap(i * 2 + e), e)
            gate(KD - 1, 1)
            act.wait_ge(slab_used, S_UP0)
            for k in range(KD):
                if k == KD - 1:
                    residual("glu", k, 1, None)
                run(xa_hi[:, k, :], h[:, k, :], ACT.Copy, scale=gain(G_FFN[0])[:, k:k + 1]
                    ).then_inc(x_hi_done["glu"], 1)

            def up(p, l, base, before, nxt):
                real = (0, META)[l]

                def tap(q, m):
                    act.wait_ge(up_evicted[p], m * 2 + (q + 1))
                    if not isinstance(m, int) or m >= 1:
                        act.wait_ge(act_done[p], m)
                    w = column(cw[:, l, 2, :], q * KF + m if isinstance(m, int) else act.snap(m + q * KF))
                    run(cbuf[:, q, real:L], ubuf[:, q, 2 + real:L + 2], ACT.Copy, scale=w).then_inc(tap_done[p], 1)

                def gate_tile(m):
                    tap(0, m)
                    act.wait_ge(conv_gate[p], m + 1)
                    run(cbuf[:, 0, real:L], cbuf[:, 0, real:L], ACT.Silu).then_inc(silu_done[p], 1)

                def val_tile(m):
                    tap(1, m)
                    act.wait_ge(act_done[p], m + 1)
                    run(tile_of(act_hi, m, real), abuf[:, real:L], ACT.Copy).then_inc(act_hi_done[p], 1)

                def tile(m, n2):
                    split_at(base, m, 2, 1, KD)
                    if isinstance(m, int) and m == 0:
                        rms(before)
                    else:
                        val_tile(m - 1 if isinstance(m, int) else act.snap(m - 1))
                    split_at(base, m, 2, 2, n2)
                    gate_tile(m)

                tile(0, KD)
                tile(1, KD)
                with act.Fori(1, KF // 2 - 1) as i:
                    for e in range(2):
                        tile(act.snap(i * 2 + e), KD)
                tile(KF - 2, KD)
                tile(KF - 1, KS)
                split_at(base + 2 * KF, 0, 2, 1, KS)
                val_tile(KF - 1)

            def down(p, base, g, nxt):
                def tile(m, par, n2):
                    if not (isinstance(m, int) and m == 0):
                        split_at(base, m, 2, 1, KS)
                        residual(p, m - 1 if isinstance(m, int) else act.snap(m - 1), 1 - par, g)
                    if p == "dn0" and isinstance(m, int) and m == KD - 2:
                        act.wait_ge(dint_set, 2)
                        run(dist[:, :, :], dint[:, :].rearrange("p (n j) -> p n j", n=NQ), ACT.Abs
                            ).then_inc(dist_abs, 1)
                    if n2:
                        split_at(base, m, 2, 2, n2)
                    if p == "dn1" and not (isinstance(m, int) and m == 0):
                        out_copy(m - 1 if isinstance(m, int) else act.snap(m - 1), 1 - par)

                tile(0, 0, KS)
                tile(1, 1, KS)
                with act.Fori(1, KD // 2 - 1) as i:
                    for e in range(2):
                        tile(act.snap(i * 2 + e), e, KS)
                tile(KD - 2, 0, KS)
                tile(KD - 1, 1, nxt)
                residual(p, KD - 1, 1, g)
                if p == "dn1":
                    out_copy(KD - 1, 1)

            def out_copy(m, par):
                act.wait_ge(ot_full, m + 1)
                o = otok[:, :, m * P:(m + 1) * P] if isinstance(m, int) else otok[:, :, bass.ds(act.snap(m * P), P)]
                run(o, slot[2 + par][:, 0, :].rearrange("p (n c) -> p n c", n=4), ACT.Copy).then_inc(ot_copied, 1)

            def attention():
                split_at(S_KV, 0, 2, 1, KD)
                rms("dn0")
                split_at(S_KV, 1, 2, 0, KD)
                for k in range(KD):
                    run(xq_hi[:, k, :], h[:, k, :], ACT.Copy, scale=gain(G_ATT)[:, k:k + 1]).then_inc(xq_hi_done, 1)
                split_at(S_KV, 1, 2, 1, KD)
                split_at(S_Q, 0, 2, 0, KD)
                act.wait_ge(v_full, 1)
                run(vtok[:, 0:4, :].rearrange("p n (a c) -> p a n c", a=2),
                    slot[2][:, :, :].rearrange("p a (n c) -> p a n c", n=4), ACT.Copy).then_inc(v_copied, 1)
                run(vtok[0:META, 4, :], slot[3][0:META, 0, 0:2 * P], ACT.Copy).then_inc(v_copied, 1)
                split_at(S_Q, 0, 2, 1, KD)

                def heads(j, hp, par, ahead):
                    for t in range(GRP):
                        three = slice(GRP * t, GRP * (t + 1))
                        act.wait_ge(m_ready, hp * GRP + (t + 1))
                        for n in range(GRP * t, GRP * (t + 1)):
                            if n == GRP * t + 1:
                                run(esnk[:, par, three], mneg[:, par, three], ACT.Exp, bias=column(sink, hp))
                            ins = run(prob[:, par, n, :], prob[:, par, n, :], ACT.Exp, bias=mneg[:, par, n:n + 1],
                                      accum_out=den[:, par, n:n + 1])
                        ins.then_inc(exp_done, 1)
                    if ahead:
                        split_at(S_Q, j, 2, 2 + par, KD)
                    act.wait_ge(pv_done, hp + 1)
                    run(tile_of(ao_hi, hp, META, L), slot[2][:, 1, :], ACT.Copy)
                    run(tile_of(ao_hi, hp, 0, META), slot[3][:, 0, 0:META], ACT.Copy).then_inc(ao_hi_done, 1)

                heads(0, 0, 0, True)
                heads(0, 1, 1, True)
                with act.Fori(1, KVH - 1) as j:
                    for e in range(2):
                        heads(j, act.snap(j * 2 + e), e, True)
                heads(KVH - 1, HP - 2, 0, True)
                heads(KVH - 1, HP - 1, 1, False)

                def o_tile(m, par):
                    if isinstance(m, int):
                        split(S_O + m + 1, 1 - par, landed(1 - par, S_O + m + 1), KD)
                    else:
                        split(m + (S_O + 1), 1 - par, m * 8 + landed(1 - par, S_O + 1), KD)
                    if not (isinstance(m, int) and m == 0):
                        residual("o", m - 1 if isinstance(m, int) else act.snap(m - 1), 1 - par, G_FFN[1])

                o_tile(0, 0)
                o_tile(1, 1)
                with act.Fori(1, KD // 2) as i:
                    for e in range(2):
                        o_tile(act.snap(i * 2 + e), e)
                residual("o", KD - 1, 1, G_FFN[1])

            up("up0", 0, S_UP0, "glu", KS)
            down("dn0", S_DN0, G_KV, KD)
            attention()
            up("up1", 1, S_UP1, "o", KS)
            down("dn1", S_DN1, None, 0)
            act.wait_ge(fin_full, 1)
            run(rinv[:, 0:4], slot[3][:, 1, 0:4], ACT.Sqrt, scale=1.0 / D, bias=eps[:, :]).then_inc(fin_rms, 1)
            act.wait_ge(fin_rinv, 1)
            for n in (0, 2):
                run(otok[:, n, :], otok[:, n, :], ACT.Copy, scale=rinv[:, n:n + 1]).then_inc(scaled_act, 1)

        @block.tensor
        def _(pe):
            mm, tr = nc.tensor.matmul, nc.tensor.transpose

            def begin(name):
                n = fill_of[name]
                if n >= 4:
                    pe.wait_ge(s5_free[n % 4], n // 4)
                return slot[n % 4]

            pe.wait_ge(consts_set, 1)
            pe.wait_ge(par_ready, 1)
            pe.wait_ge(g5_in, 16 * T)
            pe.wait_ge(rows_in, 16 * 7)
            ps = begin("par")
            for n, name in enumerate(("lbr", "lbi", "cr", "ci")):
                tr(ps[:, 0, n * PAIRS:(n + 1) * PAIRS], pm[name][0:PAIRS, :], ident[0:PAIRS, 0:PAIRS])
            for n, name in enumerate(("r", "c", "s")):
                tr(ps[:, 1, n * PAIRS:(n + 1) * PAIRS], pm[name][0:PAIRS, :], ident[0:PAIRS, 0:PAIRS])
            tr(ps[:, 0, 128:128 + G], g5row[0:G, :], ident[0:G, 0:G])
            tr(ps[:, 0, 192:192 + 5 * KD], grow[0:5 * KD, :], ident[0:5 * KD, 0:5 * KD])
            for n in range(3):
                ins = tr(ps[:, 0, 232 + n * 4 * KF:232 + (n + 1) * 4 * KF], crow[0:4 * KF, n * P:(n + 1) * P],
                         ident[0:4 * KF, 0:4 * KF])
            ins.then_inc(s5_full, 1)
            pe.wait_ge(c_in, 64)
            for r in range(2):
                ps = begin(f"c{r}")
                for k in range(KD):
                    ins = tr(ps[:, k // 4, (k % 4) * P:(k % 4 + 1) * P],
                             craw[r][:, k].rearrange("p t s -> p (t s)"), ident[:, :])
                ins.then_inc(s5_full, 1)
            pe.wait_ge(xn_ready, T)
            for b in range(8):
                ps = begin(f"u{b}")
                for n in range(8):
                    ins = tr(ps[:, n // 4, (n % 4) * NC:(n % 4 + 1) * NC],
                             xn[0:NC, 8 * b + n].rearrange("c t h -> c (t h)"), ident[0:NC, 0:NC])
                ins.then_inc(s5_full, 1)
            for b in range(8):
                copied_wait(pe, f"u{b}")

            def input_map(b):
                pe.wait_ge(win_t_ready, b + 1)
                ps = begin(f"w{b}")
                for r in range(2):
                    for q in range(4):
                        ins = tr(ps[:, r, q * P:(q + 1) * P],
                                 win_t[:, b % 2, r, q].rearrange("p t h -> p (t h)"), ident[:, :])
                ins.then_inc(s5_full, 1)

            def additions(b):
                copied_wait(pe, f"w{b}")
                ps = begin(f"v{b}")
                for q in range(4):
                    for r in range(2):
                        for t in range(2):
                            col = ((q % 2) * 2 + r) * NV
                            ins = mm(ps[t * S:(t + 1) * S, q // 2, col:col + NV],
                                     win[:, b % 2, r, q, t * S:(t + 1) * S],
                                     u5[:, 2 * (4 * b + q) + t, 0:NV], start=True, stop=True)
                ins.then_inc(s5_full, 1)

            def kernels(b):
                pe.wait_ge(cpow_ready, 2 * b + 2)
                ps = begin(f"g{b}")
                for n in range(8):
                    q = 8 * b + n
                    for r in range(2):
                        ins = mm(ps[0:2 * HC, n // 4, (n % 4) * TH:(n % 4 + 1) * TH],
                                 bpad[r][:, q].rearrange("p g h -> p (g h)"),
                                 cpow[r][:, q, 0:T, :].rearrange("p k h -> p (k h)"), start=r == 0, stop=r == 1)
                ins.then_inc(s5_full, 1)

            def outputs(k):
                pe.wait_ge(toep_in[k // 2], 32 * T)
                ps = begin(f"y{k}")
                for n in range(8):
                    g, u = 8 * k + n, 2 * k + n // 4
                    if n % 4 == 0:
                        pe.wait_ge(zpad_ready, u + 1)
                    o = ps[0:NC, n // 4, (n % 4) * TH:(n % 4 + 1) * TH]
                    mm(o, u5[:, g, :], toep[:, g, :], start=True, stop=False)
                    for r in range(2):
                        ins = mm(o, zpad[:, u % 3, (n // 2) % 2, n % 2, r, :],
                                 cpow[r][:, g // 2, 1:T + 1, :].rearrange("p k h -> p (k h)"),
                                 start=False, stop=r == 1)
                    if n == 3:
                        ins.then_inc(zpad_used, 1)
                ins.then_inc(s5_full, 1)

            def operand(k):
                copied_wait(pe, f"y{k}")
                ps = begin(f"t{k}")
                for t in range(T):
                    ins = tr(ps[:, t // 4, (t % 4) * NC:(t % 4 + 1) * NC], gy[0:NC, k % 2, t, :], ident[0:NC, 0:NC])
                ins.then_inc(s5_full, 1)

            def stream(k):
                ps = begin(f"h{k}")
                tr(ps[:, 0, 0:META], xt_meta[0:META, k * P:(k + 1) * P], ident[0:META, 0:META])
                for n in range(4):
                    col = (META, META + P, 0, P)[n]
                    ins = tr(ps[:, n // 2, col:col + P], xt[:, n * D + k * P:n * D + (k + 1) * P], ident[:, :])
                ins.then_inc(s5_full, 1)

            for b in range(8):
                input_map(b)
                additions(b)
                if b == 0:
                    copied_wait(pe, "c0")
                    copied_wait(pe, "c1")
                    pe.wait_ge(bpad_ready, 1)
                if b % 2 == 0:
                    kernels(b // 2)
                if b >= 2:
                    outputs(b - 2)
                if b >= 3:
                    operand(b - 3)
            outputs(6)
            operand(5)
            outputs(7)
            operand(6)
            pe.wait_ge(xt_in, 32)
            for k in range(4):
                stream(k)
            operand(7)
            for k in range(4, KD):
                stream(k)

            def slab(s, buf, dst, x_hi, x_lo, k0=0, nk=KD, opens=True, closes=True, ready=None, part=None,
                     tokens=ALL_TOKENS):
                start, stop = part or (0, nk)
                if start == 0:
                    pe.wait_ge(hi_done, s + 1)
                    pe.wait_ge(lo_done, s + 1)
                for k in range(start, stop):
                    if ready is not None:
                        ready(k)
                    for n, (w, xx) in enumerate(((w_hi, x_hi), (w_hi, x_lo), (w_lo, x_hi))):
                        for half, (a, b) in enumerate(tokens):
                            ins = mm(slot[dst][:, half, 0:b - a], w[:, buf, k * P:(k + 1) * P], xx[:, k0 + k, a:b],
                                     start=opens and k == 0 and n == 0, stop=closes and k == nk - 1 and n == 2)
                if stop == nk:
                    ins.then_inc(slab_used, 1)

            def operand_ready(p):
                def ready(k):
                    pe.wait_ge(x_hi_done[p], k + 1)
                    pe.wait_ge(x_lo_done[p], k + 1)
                return ready

            def statistics(p):
                pe.wait_ge(acc_done[p], KD)
                for half in range(2):
                    ins = mm(slot[3][:, half, 0:HALF], ones[:, :], acc[:, half * HALF:(half + 1) * HALF],
                             start=True, stop=True)
                ins.then_inc(stat_full[p], 1)

            def glu_ready(k):
                pe.wait_ge(glu_x_hi, k + 1)
                copied_wait(pe, f"t{k}")

            def glu_pair(m, e):
                for q in range(2):
                    if isinstance(m, int) and m < 2:
                        pe.wait_ge(s5_free[2 * e + q], N_FILLS[2 * e + q])
                    elif q == 0:
                        pe.wait_ge(glu_mul, m - 1)
                    slab(m * 2 + (S_GLU + q), q, 2 * e + q, xa_hi, xa_lo,
                         ready=glu_ready if isinstance(m, int) and m == 0 and q == 0 else None)

            glu_pair(0, 0)
            glu_pair(1, 1)
            with pe.Fori(1, KD // 2) as i:
                for e in range(2):
                    glu_pair(pe.snap(i * 2 + e), e)

            def up(p, base, before, slots_free, tokens):
                for q in range(4):
                    slots_free(q)
                    if q == 3:
                        pe.wait_ge(stat_read[before], 1)
                    slab(base + q, q % 2, q, xa_hi, xa_lo, ready=operand_ready(before) if q == 0 else None,
                         tokens=tokens)
                    if q == 0:
                        slots_free(3)
                        statistics(before)
                with pe.Fori(1, KF // 2) as i:
                    for q in range(4):
                        pe.wait_ge(up_evicted[p], i * 4 + (q - 3))
                        slab(i * 4 + (base + q), q % 2, q, xa_hi, xa_lo, tokens=tokens)

            def down(p, base, before, tokens, hook=None):
                def act_ready(k):
                    pe.wait_ge(act_hi_done[before], KS + k + 1)
                    pe.wait_ge(act_lo_done[before], KS + k + 1)

                def tile(m, e):
                    if isinstance(m, int) and m < 2:
                        pe.wait_ge(up_evicted[before], 2 * KF - 3 + e)
                    else:
                        pe.wait_ge(h_done[p], m - 1)
                    if isinstance(m, int) and m == 0:
                        pe.wait_ge(act_hi_done[before], KS)
                        pe.wait_ge(act_lo_done[before], KS)
                    slab(m * 2 + base, 0, e, act_hi, act_lo, 0, KS, True, False, tokens=tokens)
                    slab(m * 2 + (base + 1), 1, e, act_hi, act_lo, KS, KS, False, True, tokens=tokens,
                         ready=act_ready if isinstance(m, int) and m == 0 else None)
                    if hook is not None:
                        hook(m, e)

                tile(0, 0)
                tile(1, 1)
                with pe.Fori(1, KD // 2) as i:
                    for e in range(2):
                        tile(pe.snap(i * 2 + e), e)

            def attention():
                for q in range(4):
                    if q < 2:
                        pe.wait_ge(h_done["dn0"], KD - 1 + q)
                    if q == 3:
                        pe.wait_ge(stat_read["dn0"], 1)
                    slab(S_KV + q, q % 2, q, xa_hi, xa_lo, ready=operand_ready("dn0") if q == 0 else None)
                    if q == 0:
                        statistics("dn0")

                def q_slab(hp, e, first=False, part=None):
                    def ready(k):
                        pe.wait_ge(xq_hi_done, k + 1)
                        pe.wait_ge(xq_lo_done, k + 1)
                    if first:
                        pe.wait_ge(kv_evicted, 1)
                    elif part is None or part[0] == 0:
                        pe.wait_ge(q_evicted, hp)
                    slab(hp + S_Q, e, 0, xq_hi, xq_lo, ready=ready if first else None, part=part,
                         tokens=Q_TOKENS)

                q_slab(0, 0, True)
                pe.wait_ge(kv_evicted, 4)
                for a in range(2):
                    for n in range(4):
                        tr(slot[2][:, a, n * P:(n + 1) * P], kvt[:, 2 + a, META + n * P:META + (n + 1) * P],
                           ident[:, :])
                    ins = tr(slot[3][0:META, 0, a * P:(a + 1) * P], kvt[:, 2 + a, 0:META], ident[:, :])
                ins.then_inc(v_full, 1)
                pe.wait_ge(v_copied, 2)

                bank = [slot[1][:, 0, :], slot[1][:, 1, :], slot[2][:, 0, :]]
                o_real, o_meta = slot[2][:, 1, :], slot[3][:, 0, :]

                def heads(j, hp, e, ahead):
                    peeled = isinstance(hp, int)
                    for t in range(GRP):
                        for n in range(GRP):
                            ins = mm(bank[t][:, n * KEYS:(n + 1) * KEYS],
                                     qt[:, e, GRP * t + n].rearrange("p x f -> p (x f)"), kcur[:, GRP * t + n, :],
                                     start=True, stop=True)
                        ins.then_inc(scores_done, 1)
                    if ahead:
                        q_slab(hp + 1, 1 - e, part=(0, Q_PART))

                    else:
                        pe.wait_ge(q_evicted, HP)
                        pe.wait_ge(ao_hi_done, HP - 1)
                        pe.wait_ge(ao_lo_done, HP - 1)
                        slab(S_O, 0, 0, ao_hi, ao_lo, tokens=LIVE_TOKENS, part=(0, HP - 1))

                    def transposes(t):
                        pe.wait_ge(p_ready, hp * GRP + (t + 1))
                        for n in range(GRP):
                            tr(bank[t][:, n * P:(n + 1) * P], prob[:, e, GRP * t + n, 0:BAND], ident[:, :])
                        tr(bank[t][0:GRP * META, GRP * P:(GRP + 1) * P],
                           probm[:, e, GRP * t:GRP * (t + 1), :].rearrange("p n j -> p (n j)"), ident[:, :]
                           ).then_inc(pt_full, 1)

                    def product(t):
                        pe.wait_ge(pt_copied, hp * GRP + (t + 1))
                        for n in range(GRP):
                            blk = GRP * t + n
                            for half in range(2):
                                part = slice(half * HD, (half + 1) * HD)
                                o = o_real[part, blk * CH:(blk + 1) * CH] if blk < NCH else o_meta[part, 0:CH]
                                if blk < NCH:
                                    mm(o, vcur[:, blk, :], pt[:, blk, part], start=True, stop=False)
                                ins = mm(o, vmet[:, n, :], ptm[:, t, part],
                                         start=blk == NCH, stop=True)
                        return ins

                    transposes(0)
                    transposes(1)
                    if ahead:
                        q_slab(hp + 1, 1 - e, part=(Q_PART, KD))
                    transposes(2)
                    if not peeled or hp >= 1:
                        pe.wait_ge(ao_lo_done, hp)
                    pe.wait_ge(v_in, j * 80 + 80)
                    product(0)
                    product(1)
                    if ahead:
                        pe.wait_ge(q_evicted, hp + 2)
                        if e == 1:
                            pe.wait_ge(k_in, j * 96 + 192)
                    product(2).then_inc(pv_done, 1)

                pe.wait_ge(q_evicted, 1)
                pe.wait_ge(k_in, 96)
                heads(0, 0, 0, True)
                heads(0, 1, 1, True)
                with pe.Fori(1, KVH - 1) as j:
                    for e in range(2):
                        heads(j, pe.snap(j * 2 + e), e, True)
                heads(KVH - 1, HP - 2, 0, True)
                heads(KVH - 1, HP - 1, 1, False)

                def o_tile(m, e):
                    if isinstance(m, int) and m == 0:
                        pe.wait_ge(ao_hi_done, HP)
                        pe.wait_ge(ao_lo_done, HP)
                    elif isinstance(m, int) and m == 1:
                        pe.wait_ge(pt_copied, GRP * HP)
                    else:
                        pe.wait_ge(h_done["o"], m - 1)
                    slab(m + S_O, e, e, ao_hi, ao_lo, tokens=LIVE_TOKENS,
                         part=(HP - 1, HP) if isinstance(m, int) and m == 0 else None)

                o_tile(0, 0)
                o_tile(1, 1)
                with pe.Fori(1, KD // 2) as i:
                    for e in range(2):
                        o_tile(pe.snap(i * 2 + e), e)

            up("up0", S_UP0, "glu", lambda q: pe.wait_ge(glu_mul, KD - 1 + q // 2), ALL_TOKENS)
            down("dn0", S_DN0, "up0", ALL_TOKENS)
            attention()
            up("up1", S_UP1, "o", lambda q: pe.wait_ge(h_done["o"], KD - 1 + min(q, 1)), LIVE_TOKENS)
            def out_tile(m, e):
                pe.wait_ge(hg_done, m + 1)
                if isinstance(m, int) and m < 2:
                    pe.wait_ge(up_evicted["up1"], 2 * KF - 1 + m)
                else:
                    pe.wait_ge(ot_copied, m - 1)
                for n in range(4):
                    ins = tr(slot[2 + e][:, 0, n * P:(n + 1) * P], sig[:, e, META + n * P:META + (n + 1) * P],
                             ident[:, :])
                ins.then_inc(ot_full, 1)

            def hook(m, e):
                if isinstance(m, int):
                    if m >= 1:
                        out_tile(m - 1, 1 - e)
                else:
                    out_tile(pe.snap(m - 1), 1 - e)

            down("dn1", S_DN1, "up1", REAL_TOKENS, hook)
            out_tile(KD - 1, 1)
            pe.wait_ge(acc_done["dn1"], KD)
            for n in range(4):
                ins = mm(slot[3][:, 1, n:n + 1], acc[:, META + n * P:META + (n + 1) * P], ones[:, 0:1],
                         start=True, stop=True)
            ins.then_inc(fin_full, 1)

        @block.vector
        def _(dve):
            chain = Chain(dve, dve_chain)
            tt, ts, stt = nc.vector.tensor_tensor, nc.vector.tensor_scalar, nc.vector.scalar_tensor_tensor
            copy = nc.vector.tensor_copy
            link = chain.link
            LN2_HI, LN2_LO = 0.693359375, -2.12194440e-4
            PI2_A, PI2_B = 6.28125, 0.00193500518798828125
            PI2_C = float(2 * np.pi - PI2_A - PI2_B)
            PI_IN = 3.1415925

            def exp_small(o, v, n, f, q, whole):
                link(ts(v, v, -87.0, 88.0, ALU.max, ALU.min))
                link(ts(n, v, float(1 / np.log(2.0)), MAGIC, ALU.mult, ALU.add))
                link(ts(n, n, MAGIC, None, ALU.subtract))
                link(stt(f, n, -LN2_HI, v, ALU.mult, ALU.add))
                link(stt(f, n, -LN2_LO, f, ALU.mult, ALU.add))
                link(ts(q, f, 1.0 / 5040, None, ALU.mult))
                for c in (1.0 / 720, 1.0 / 120, 1.0 / 24, 1.0 / 6, 0.5, 1.0):
                    link(stt(q, q, c, f, ALU.add, ALU.mult))
                link(ts(n, n, 127.0, None, ALU.add))
                link(copy(whole, n))
                link(ts(whole, whole, 23, None, ALU.logical_shift_left))
                link(stt(o, q, 1.0, whole.bitcast(F32), ALU.add, ALU.mult))

            def cmul(o, a, b, tmp):
                tt(o[0], a[0], b[0], ALU.mult)
                tt(tmp[0], a[1], b[1], ALU.mult)
                tt(o[1], a[0], b[1], ALU.mult)
                chain.did(tt(tmp[1], a[1], b[0], ALU.mult))
                chain.sync()
                tt(o[0], o[0], tmp[0], ALU.subtract)
                chain.did(tt(o[1], o[1], tmp[1], ALU.add))
                chain.sync()

            for hp in range(HP):
                for half in range(2):
                    nc.vector.memset(negslope[half * CH:(half + 1) * CH, hp:hp + 1],
                                     -float(2.0 ** (-8.0 * (2 * hp + half + 1) / HEADS)))

            dve.wait_ge(par_in, 48)
            a = {n: t[0:PAIRS, :] for n, t in pm.items()}
            pair = lambda t: t.rearrange("p (t s) -> p t s", t=2)
            exp_small(stp[0:PAIRS, :], lst[0:PAIRS, :], se["a"][0:PAIRS, :], se["b"][0:PAIRS, :], se["c"][0:PAIRS, :],
                      sei[0:PAIRS, :])
            step = stp[0:PAIRS, :, None].to_broadcast([PAIRS, 2, S])
            link(ts(a["lr"], a["lr"], -1e-4, None, ALU.min))
            tt(pair(a["ar"]), pair(a["lr"]), step, ALU.mult)
            link(tt(pair(a["th"]), pair(a["li"]), step, ALU.mult))
            link(ts(a["n"], a["th"], float(1 / (2 * np.pi)), MAGIC, ALU.mult, ALU.add))
            link(ts(a["n"], a["n"], MAGIC, None, ALU.subtract))
            link(stt(a["a"], a["n"], -PI2_A, a["th"], ALU.mult, ALU.add))
            link(stt(a["a"], a["n"], -PI2_B, a["a"], ALU.mult, ALU.add))
            link(stt(a["a"], a["n"], -PI2_C, a["a"], ALU.mult, ALU.add))
            link(ts(a["b"], a["a"], float(np.pi / 2), None, ALU.add))
            link(ts(a["d"], a["b"], float(np.pi), -float(2 * np.pi), ALU.is_gt, ALU.mult))
            link(tt(a["b"], a["b"], a["d"], ALU.add))
            ts(a["b"], a["b"], -PI_IN, PI_IN, ALU.max, ALU.min)
            ts(a["a"], a["a"], -PI_IN, PI_IN, ALU.max, ALU.min).then_inc(angles_ready, 1)
            exp_small(a["r"], a["ar"], a["n"], a["cr"], a["ci"], pi[0:PAIRS, :])
            dve.wait_ge(sincos_ready, 1)
            tt(a["lbr"], a["r"], a["c"], ALU.mult)
            tt(a["lbi"], a["r"], a["s"], ALU.mult)
            tt(a["d"], a["lr"], a["lr"], ALU.mult)
            link(tt(a["th"], a["li"], a["li"], ALU.mult))
            ts(a["n"], a["lbr"], 1.0, None, ALU.subtract)
            link(tt(a["d"], a["d"], a["th"], ALU.add))
            nc.vector.reciprocal(a["d"], a["d"])
            tt(a["cr"], a["n"], a["lr"], ALU.mult)
            tt(a["a"], a["lbi"], a["li"], ALU.mult)
            tt(a["ci"], a["lbi"], a["lr"], ALU.mult)
            link(tt(a["b"], a["n"], a["li"], ALU.mult))
            tt(a["cr"], a["cr"], a["a"], ALU.add)
            link(tt(a["ci"], a["ci"], a["b"], ALU.subtract))
            tt(a["cr"], a["cr"], a["d"], ALU.mult)
            tt(a["ci"], a["ci"], a["d"], ALU.mult).then_inc(par_ready, 1)
            dve.wait_ge(ssq5_ready, 1)
            nc.vector.reciprocal(rst5[0:NC, :], ssq5[0:NC, :]).then_inc(rst5_ready, 1)
            full_wait(dve, "par")
            ps = fslot("par")
            for r in range(2):
                copy(lpow[r][:, 1, :], ps[:, 0, r * PAIRS:(r + 1) * PAIRS])
                copy(coef[r][:, :], ps[:, 0, (2 + r) * PAIRS:(3 + r) * PAIRS])
                nc.vector.memset(lpow[r][:, 0, :], 1.0 - r)
            copy(gain5[:, :], ps[:, 0, 128:128 + G])
            copy(rho[:, :], ps[:, 1, 0:PAIRS])
            copy(ph[0], ps[:, 1, PAIRS:3 * PAIRS].rearrange("p (r q) -> p r q", r=2))
            copy(gains[:, :], ps[:, 0, 192:192 + 5 * KD])
            for half in range(2):
                part = slice(half * CH, (half + 1) * CH)
                copy(sink[part, :], sinkrow[part, :].rearrange("p (a b) -> p a b", b=2)[:, :, half])
            last = copy(conv_w[:, :], ps[:, 0, 232:232 + 12 * KF])
            frees(last, "par")
            copied_wait(dve, "par")
            for n in (1, 2, 4):
                tmp = [ltmp[r][:, 0:n * PAIRS].rearrange("p (k q) -> p k q", k=n) for r in range(2)]
                cmul([lpow[r][:, n + 1:2 * n + 1, :] for r in range(2)], [lpow[r][:, 1:n + 1, :] for r in range(2)],
                     [lpow[r][:, n:n + 1, :].to_broadcast([P, n, PAIRS]) for r in range(2)], tmp)
            tt(rho[:, :], rho[:, :], rho[:, :], ALU.mult).then_inc(lpow_ready, 1)
            dve.wait_ge(lpow_ready, 1)
            dve.wait_ge(b_in, 32)
            cmul([bbar[r][:, :, :] for r in range(2)],
                 [coef[r][:, :, None].to_broadcast([P, PAIRS, HC]) for r in range(2)], braw,
                 [ltmp[r][:, :].rearrange("p (q h) -> p q h", q=PAIRS) for r in range(2)])

            dve.wait_ge(bpad_zero, 1)
            for r in range(2):
                for g2 in range(2):
                    part = slice(g2 * S, (g2 + 1) * S)
                    ins = copy(bpad[r][part, :, g2, :], bbar[r][part, :, :])
            ins.then_inc(bpad_ready, 1)

            def in_map(b):
                if b >= 2:
                    full_wait(dve, f"w{b - 2}")
                lp = [lpow[r][:, T - 1::-1, 4 * b:4 * b + 4].rearrange("p t q -> p q t")[:, :, :, None]
                      .to_broadcast([P, 4, T, HC]) for r in range(2)]
                bb = [bbar[r][:, 4 * b:4 * b + 4, None, :].to_broadcast([P, 4, T, HC]) for r in range(2)]
                tmp = [dtmp[r][:, 0:512].rearrange("p (q t h) -> p q t h", q=4, t=T) for r in range(2)]
                o = [win_t[:, b % 2, r] for r in range(2)]
                tt(o[0], lp[0], bb[0], ALU.mult)
                tt(tmp[0], lp[1], bb[1], ALU.mult)
                tt(o[1], lp[0], bb[1], ALU.mult)
                link(tt(tmp[1], lp[1], bb[0], ALU.mult))
                tt(o[0], o[0], tmp[0], ALU.subtract)
                tt(o[1], o[1], tmp[1], ALU.add).then_inc(win_t_ready, 1)
                dve.wait_ge(win_t_ready, b + 1)

            dve.wait_ge(xn_ready, T)
            in_map(0)
            in_map(1)
            for n in range(3):
                if n < 2:
                    chain.did(tt(rho[:, :], rho[:, :], rho[:, :], ALU.mult))
                src = [ph[n % 2][:, r, :] for r in range(2)]
                dst = [ph[1 - n % 2][:, r, :] for r in range(2)] if n < 2 else [phase[:, :, r, 0] for r in range(2)]
                cmul(dst, src, src, [dtmp[r][:, 0:PAIRS] for r in range(2)])

            def unit(e, n):
                w2 = dtmp[0][:, 0:2 * n].rearrange("p (q r) -> p q r", r=2)
                f = dtmp[1][:, 0:n]
                link(tt(w2, e, e, ALU.mult))
                link(tt(w2[:, :, 0], w2[:, :, 0], w2[:, :, 1], ALU.add))
                link(ts(f, w2[:, :, 0], -0.5, 1.5, ALU.mult, ALU.add))
                link(tt(e, e, f[:, :, None].to_broadcast([P, n, 2]), ALU.mult))
                return w2[:, :, 0]

            size2 = unit(phase[:, :, :, 0], PAIRS)
            link(ts(size2, size2, 0.5, 0.5, ALU.mult, ALU.add))
            tt(rho[:, :], rho[:, :], size2, ALU.mult).then_inc(phase_1, 1)
            dve.wait_ge(phase_1, 1)

            def phases(q0):
                pq = phase[:, q0:q0 + PAIRS // 2]
                n = 1
                while n < NV:
                    m = min(n, NV - n)
                    if n >= 8:
                        unit(pq[:, :, :, n - 1], PAIRS // 2)
                    cmul([pq[:, :, r, n:n + m] for r in range(2)], [pq[:, :, r, 0:m] for r in range(2)],
                         [pq[:, :, r, n - 1:n].to_broadcast([P, PAIRS // 2, m]) for r in range(2)],
                         [dtmp[r][:, 0:m * PAIRS // 2].rearrange("p (q c) -> p q c", c=m) for r in range(2)])
                    n += m

            ab = [dtmp[r][:, :].rearrange("p (q r c) -> p q r c", q=4, r=2) for r in range(2)]

            def turn(q0, n):
                return [phase[:, q0:q0 + n, r, None, :].to_broadcast([P, n, 2, NV]) for r in range(2)]

            def scan(b):
                name, z = f"v{b}", zrot[:, b % 2]
                full_wait(dve, name)
                for a in range(2):
                    cs, q2 = turn(4 * b + 2 * a, 2), slice(2 * a, 2 * a + 2)
                    v = fslot(name)[:, a, 0:4 * NV].rearrange("p (q r c) -> p q r c", q=2, r=2)
                    tt(ab[0][:, q2], v, cs[0], ALU.mult)
                    ins = tt(ab[1][:, q2], v[:, :, 1::-1, :], cs[1], ALU.mult)
                frees(ins, name)
                copied_wait(dve, name)
                tt(z[:, :, 0], ab[0][:, :, 0], ab[1][:, :, 0], ALU.add)
                link(tt(z[:, :, 1], ab[0][:, :, 1], ab[1][:, :, 1], ALU.subtract))
                for q in range(4):
                    for r in range(2):
                        ins = nc.vector.tensor_tensor_scan(
                            z[:, q, r, :], rho[:, 4 * b + q:4 * b + q + 1].to_broadcast([P, NV]), z[:, q, r, :],
                            0.0, ALU.mult, ALU.add)
                chain.did(ins)

            def states(b):
                z, cs = zrot[:, b % 2], turn(4 * b, 4)
                chain.sync()
                tt(ab[0], z, cs[0], ALU.mult)
                link(tt(ab[1], z[:, :, 1::-1, :], cs[1], ALU.mult))
                for u in (2 * b, 2 * b + 1):
                    if u >= 3:
                        if (u - 3) % 2 == 0:
                            dve.wait_ge(zpad_used, (u - 3) // 2 + 1)
                        else:
                            full_wait(dve, f"y{(u - 3) // 2}")
                    q2 = slice(2 * (u % 2), 2 * (u % 2) + 2)
                    for g2 in range(2):
                        part = slice(g2 * S, (g2 + 1) * S)
                        o = zpad[part, u % 3, :, g2]
                        tt(o[:, :, 0, 1:NC], ab[0][part, q2, 0], ab[1][part, q2, 0], ALU.subtract)
                        ins = tt(o[:, :, 1, 1:NC], ab[0][part, q2, 1], ab[1][part, q2, 1], ALU.add)
                    ins.then_inc(zpad_ready, 1)
                dve.wait_ge(zpad_ready, 2 * b + 2)

            def glu_x_low(k):
                name = f"t{k}"
                dve.wait_ge(glu_x_hi, k + 1)
                for half in range(2):
                    view = lambda t: t[:, k, :].rearrange("p (c b t) -> p b t c", b=2, t=T // 2)[:, half]
                    ins = tt(view(xa_lo), fslot(name)[:, half, 0:4 * NC].rearrange("p (t c) -> p t c", t=4),
                             f32(view(xa_hi)), ALU.subtract)
                frees(ins, name)

            def stream(k):
                name = f"h{k}"
                full_wait(dve, name)
                copy(h[:, k, 0:META + 2 * P], fslot(name)[:, 0, 0:META + 2 * P])
                frees(copy(h[:, k, META + 2 * P:L], fslot(name)[:, 1, 0:2 * P]), name)

            phases(0)
            dve.wait_ge(zpad_zero, 1)
            for b in range(8):
                if b == 1:
                    phases(PAIRS // 2)
                scan(b)
                if b + 2 < POOL_MAPS:
                    in_map(b + 2)
                if b >= 3:
                    glu_x_low(b - 3)
                states(b)
            glu_x_low(5)
            glu_x_low(6)
            for k in (1, 3):
                stream(k)
            glu_x_low(7)
            for k in (5, 7):
                stream(k)

            def update(p, m, e, g, last_slab):
                dve.wait_ge(slab_used, last_slab)
                first, product = {"dn0": (0, acc_of), "o": (LIVE, live_of), "dn1": (META, real_of)}[p]
                hm = halves(tile_of(h, m, first))
                tt(hm, product(e), hm, ALU.add).then_inc(h_done[p], 1)
                if g is not None:
                    dve.wait_ge(x_hi_done[p], m + 1)
                    stt(tile_of(xa_lo, m), tile_of(h, m), column(gain(g), m), f32(tile_of(xa_hi, m)),
                        ALU.mult, ALU.subtract).then_inc(x_lo_done[p], 1)

            def inverse_rms(p, scaled=False):
                dve.wait_ge(stat_read[p], 1)
                nc.vector.reciprocal(rinv[:, :], rinv[:, :]).then_inc(rinv_ready[p], 1)
                dve.wait_ge(rinv_ready[p], 1)
                if scaled:
                    ts(rinv8[:, :], rinv[:, :], HD ** -0.5, None, ALU.mult).then_inc(rinv_ready[p], 1)

            def loop_2(n, body):
                body(0, 0)
                body(1, 1)
                k0 = chain.k
                with dve.Fori(1, n // 2) as i:
                    for e in range(2):
                        body(dve.snap(i * 2 + e), e)
                assert chain.k == k0, "the chain does not count here"

            def glu(m, e):
                dve.wait_ge(glu_sig, m + 1)
                tt(halves(sig[:, e, :]), acc_of(2 * e), halves(sig[:, e, :]), ALU.mult).then_inc(glu_mul, 1)
                dve.wait_ge(glu_mul, m + 1)
                tt(tile_of(h, m), tile_of(h, m), sig[:, e, :], ALU.add).then_inc(h_done["glu"], 1)

            for k in range(KD):
                copied_wait(dve, f"h{k}")
            loop_2(KD, glu)

            def up(p, l, before):
                inverse_rms(before)
                per = 3

                def tile(m):
                    w = lambda q, t: column(cw[:, l, t, :], m if q == 0 else (m + KF if isinstance(m, int)
                                                                              else dve.snap(m + KF)))
                    first = isinstance(m, int) and m == 0
                    for q in range(2):
                        dve.wait_ge(slab_used, m * 2 + ((S_UP0, S_UP1)[l] + q + 1))
                        tt(halves(ubuf[:, q, 2 + live:L + 2]), acc_of_q(q, m), halves(rinv[:, live:L]), ALU.mult
                           ).then_inc(up_evicted[p], 1)
                        dve.wait_ge(tap_done[p], m * 2 + (q + 1))
                        link(stt(cbuf[:, q, real:L], ubuf[:, q, 1 + real:L + 1], w(q, 1), cbuf[:, q, real:L],
                                 ALU.mult, ALU.add))
                        ins = stt(cbuf[:, q, real:L], ubuf[:, q, real:L], w(q, 0), cbuf[:, q, real:L],
                                  ALU.mult, ALU.add)
                        if q == 0:
                            ins.then_inc(conv_gate[p], 1)
                        else:
                            link(ins)
                    dve.wait_ge(silu_done[p], m + 1)
                    if not first:
                        dve.wait_ge(act_hi_done[p], m)
                        dve.wait_ge(act_lo_done[p], m)
                    tt(abuf[:, real:L], cbuf[:, 0, real:L], cbuf[:, 1, real:L], ALU.mult).then_inc(act_done[p], 1)

                par = [0]

                live, real = ((0, 0), (LIVE, META))[l]

                def acc_of_q(q, m):
                    return (acc_of, live_of)[l](2 * par[0] + q)

                dve.wait_ge(ubuf_zero, l + 1)
                for m in range(2):
                    par[0] = m
                    tile(m)
                with dve.Fori(1, KF // 2) as i:
                    chain.loop(i, 2 * per)
                    for e in range(2):
                        par[0] = e
                        tile(dve.snap(i * 2 + e))
                chain.leave(KF // 2 - 1, 2 * per)

            def attention():
                inverse_rms("dn0", scaled=True)
                dve.wait_ge(rinv_ready["dn0"], 2)
                for q in range(4):
                    dve.wait_ge(slab_used, S_KV + q + 1)
                    tt(halves(kvt[:, q, :]), acc_of(q), halves(rinv[:, :]), ALU.mult).then_inc(kv_evicted, 1)
                    for k in range(2 * q, 2 * q + 2):
                        dve.wait_ge(xq_hi_done, k + 1)
                        stt(xq_lo[:, k, :], h[:, k, :], gain(G_ATT)[:, k:k + 1], f32(xq_hi[:, k, :]),
                            ALU.mult, ALU.subtract).then_inc(xq_lo_done, 1)
                dve.wait_ge(dist_set, 1)
                bank = [slot[1][:, 0, :], slot[1][:, 1, :], slot[2][:, 0, :]]

                def q_out(hp, e):
                    dve.wait_ge(slab_used, hp + (S_Q + 1))
                    if not isinstance(hp, int) or hp >= 2:
                        dve.wait_ge(scores_done, (hp - 1) * GRP)
                    for x in range(2):
                        part = slice(x * HD, (x + 1) * HD)
                        tt(qt[part, e, 0:NCH, x, :].rearrange("p (a n) f -> p a n f", a=2),
                           slot[0][part, :, Q_LEAD:Q_LEAD + SEQ // 2].rearrange("p a (n f) -> p a n f", f=CH),
                           rinv8[part, META:L].rearrange("p (a n f) -> p a n f", a=2, f=CH), ALU.mult)
                        ins = tt(qt[part, e, NCH, x, LIVE:META], slot[0][part, 0, 0:Q_LEAD],
                                 rinv8[part, LIVE:META], ALU.mult)
                    ins.then_inc(q_evicted, 1)

                def heads(hp, e, ahead):
                    def scores(t):
                        three = slice(GRP * t, GRP * (t + 1))
                        dve.wait_ge(scores_done, hp * GRP + (t + 1))
                        s = prob[:, e, three, :]
                        link(stt(s, dist[:, three, :], column(negslope, hp),
                                 bank[t][:, 0:GRP * KEYS].rearrange("p (n j) -> p n j", n=GRP), ALU.mult, ALU.add))
                        link(nc.vector.reduce_max(mneg[:, e, three], s, AX.X))
                        ts(mneg[:, e, three], mneg[:, e, three], column(sink, hp), -1.0, ALU.max, ALU.mult
                           ).then_inc(m_ready, 1)

                    def denominators(t):
                        three = slice(GRP * t, GRP * (t + 1))
                        dve.wait_ge(exp_done, hp * GRP + (t + 1))
                        link(tt(rden[:, e, three], den[:, e, three], esnk[:, e, three], ALU.add))
                        nc.vector.reciprocal(rden[:, e, three], rden[:, e, three]).then_inc(rden_ready, 1)

                    scores(0)
                    scores(1)
                    denominators(0)
                    scores(2)
                    denominators(1)
                    denominators(2)
                    for t in range(GRP):
                        if ahead and t == GRP - 1:
                            q_out(hp + 1 if isinstance(hp, int) else dve.snap(hp + 1), 1 - e)
                        three = slice(GRP * t, GRP * (t + 1))
                        dve.wait_ge(pt_full, hp * GRP + (t + 1))
                        if t == 0 and (not isinstance(hp, int) or hp >= 1):
                            dve.wait_ge(pv_done, hp)
                        copy(pt[:, three, :], bank[t][:, 0:GRP * P].rearrange("p (n q) -> p n q", n=GRP))
                        copy(ptm[0:GRP * META, t, :], bank[t][0:GRP * META, GRP * P:(GRP + 1) * P]
                             ).then_inc(pt_copied, 1)
                    dve.wait_ge(ao_hi_done, hp + 1)
                    tt(tile_of(ao_lo, hp, META, L), slot[2][:, 1, :], f32(tile_of(ao_hi, hp, META, L)), ALU.subtract)
                    tt(tile_of(ao_lo, hp, 0, META), slot[3][:, 0, 0:META], f32(tile_of(ao_hi, hp, 0, META)),
                       ALU.subtract).then_inc(ao_lo_done, 1)

                dve.wait_ge(pads_zero, 1)
                q_out(0, 0)
                heads(0, 0, True)
                heads(1, 1, True)
                per = 2 * (GRP * 3)
                with dve.Fori(1, KVH - 1) as j:
                    chain.loop(j, per)
                    for e in range(2):
                        heads(dve.snap(j * 2 + e), e, True)
                chain.leave(KVH - 2, per)
                heads(HP - 2, 0, True)
                heads(HP - 1, 1, False)
                loop_2(KD, lambda m, e: update("o", m, e, G_FFN[1], m + (S_O + 1)))

            for k in range(KD):
                dve.wait_ge(x_hi_done["glu"], k + 1)
                stt(xa_lo[:, k, :], h[:, k, :], gain(G_FFN[0])[:, k:k + 1], f32(xa_hi[:, k, :]),
                    ALU.mult, ALU.subtract).then_inc(x_lo_done["glu"], 1)
            up("up0", 0, "glu")
            loop_2(KD, lambda m, e: update("dn0", m, e, G_KV, m * 2 + (S_DN0 + 2)))
            attention()
            up("up1", 1, "o")
            def out_update(m, e):
                update("dn1", m, e, None, m * 2 + (S_DN1 + 2))
                dve.wait_ge(h_done["dn1"], m + 1)
                if not isinstance(m, int) or m >= 2:
                    dve.wait_ge(ot_full, m - 1)
                ts(sig[:, e, :], tile_of(h, m), column(gain(G_FIN), m), None, ALU.mult).then_inc(hg_done, 1)

            loop_2(KD, out_update)
            dve.wait_ge(fin_rms, 1)
            nc.vector.reciprocal(rinv[:, 0:4], rinv[:, 0:4]).then_inc(fin_rinv, 1)
            dve.wait_ge(fin_rinv, 1)
            dve.wait_ge(ot_copied, KD)
            for n in (1, 3):
                ts(otok[:, n, :], otok[:, n, :], rinv[:, n:n + 1], None, ALU.mult).then_inc(scaled_dve, 1)

        @block.gpsimd
        def _(pool):
            chain = Chain(pool, pool_chain)
            link = chain.link
            tt, ts, memset = nc.gpsimd.tensor_tensor, nc.gpsimd.tensor_scalar, nc.gpsimd.memset

            link(memset(ident[:, :], 0.0))
            nc.gpsimd.affine_select(out=ident[:, :], in_=ident[:, :], compare_op=ALU.not_equal, fill=1.0, base=0,
                                    pattern=[[-1, P]], channel_multiplier=1)
            memset(ones[:, :], 1.0)
            memset(eps[:, :], EPS).then_inc(consts_set, 1)
            for r in range(2):
                ins = memset(bpad[r], 0.0)
            ins.then_inc(bpad_zero, 1)
            pool.wait_ge(d_in, 32)
            pool.wait_ge(consts_set, 1)
            link(tt(diag2[0:2 * HC, :], ident[0:2 * HC, 0:HC], ident[0:2 * HC, HC:2 * HC], ALU.add))
            tt(dskip[0:2 * HC], drow[0:2 * HC], diag2[0:2 * HC, None, :].to_broadcast([2 * HC, PAIRS, HC]), ALU.mult
               ).then_inc(dskip_ready, 1)
            pool.wait_ge(lpow_ready, 1)
            copied_wait(pool, "c0")
            copied_wait(pool, "c1")
            def output_maps(b):
                q4 = slice(4 * b, 4 * b + 4)
                c0 = [cpow[r][:, q4, 0, None, :].to_broadcast([P, 4, T, HC]) for r in range(2)]
                lp = [lpow[r][:, 1:T + 1, q4].rearrange("p k q -> p q k")[:, :, :, None].to_broadcast([P, 4, T, HC])
                      for r in range(2)]
                o = [cpow[r][:, q4, 1:T + 1, :] for r in range(2)]
                tmp = ptmp[:, :].rearrange("p (q k h) -> p q k h", q=4, k=T)
                tt(o[0], c0[0], lp[0], ALU.mult)
                link(tt(tmp, c0[1], lp[1], ALU.mult))
                tt(o[1], c0[1], lp[0], ALU.mult)
                link(tt(o[0], o[0], tmp, ALU.add))
                link(tt(tmp, c0[0], lp[1], ALU.mult))
                tt(o[1], o[1], tmp, ALU.subtract).then_inc(cpow_ready, 1)
                pool.wait_ge(cpow_ready, b + 1)

            def input_maps(b):
                full_wait(pool, f"w{b - 2}")
                lp = [lpow[r][:, T - 1::-1, 4 * b:4 * b + 4].rearrange("p t q -> p q t")[:, :, :, None]
                      .to_broadcast([P, 4, T, HC]) for r in range(2)]
                bb = [bbar[r][:, 4 * b:4 * b + 4, None, :].to_broadcast([P, 4, T, HC]) for r in range(2)]
                o = [win_t[:, b % 2, r] for r in range(2)]
                tmp = ptmp[:, :].rearrange("p (q k h) -> p q k h", q=4, k=T)
                tt(o[0], lp[0], bb[0], ALU.mult)
                link(tt(tmp, lp[1], bb[1], ALU.mult))
                tt(o[1], lp[0], bb[1], ALU.mult)
                link(tt(o[0], o[0], tmp, ALU.subtract))
                link(tt(tmp, lp[1], bb[0], ALU.mult))
                pool.wait_ge(win_t_ready, b)
                tt(o[1], o[1], tmp, ALU.add).then_inc(win_t_ready, 1)
                pool.wait_ge(win_t_ready, b + 1)

            def skip(b):
                copied_wait(pool, f"g{b}")
                kd = kern[0:2 * HC, b % 2, :, 0:HC]
                tt(kd, kd, dskip[0:2 * HC, 8 * b:8 * (b + 1), :], ALU.add).then_inc(kern_d_ready, 1)

            output_maps(0)
            output_maps(1)
            pool.wait_ge(bpad_ready, 1)
            memset(zpad, 0.0).then_inc(zpad_zero, 1)
            for b in range(8):
                copied_wait(pool, f"u{b}")
            memset(toep[:, :, :], 0.0).then_inc(toep_zero, 1)
            pool.wait_ge(dskip_ready, 1)
            for b in range(2, 8):
                output_maps(b)
                if b % 2 == 0:
                    skip(b // 2 - 1)
            for b in range(POOL_MAPS, 8):
                input_maps(b)
            skip(3)

            def low(s, buf, nk):
                pool.wait_ge(hi_done, s + 1)
                tt(w_lo[:, buf, 0:nk * P], raw[:, buf, 0:nk * P], f32(w_hi[:, buf, 0:nk * P]), ALU.subtract
                   ).then_inc(lo_done, 1)

            def add_square(p, m, par):
                pool.wait_ge(sq_done[p], m + 1)
                if isinstance(m, int) and m == 0:
                    pool.wait_ge(acc_zero[p], 1)
                else:
                    pool.wait_ge(acc_done[p], m)
                tt(acc[:, :], acc[:, :], sq[:, par, :], ALU.add).then_inc(acc_done[p], 1)

            def loop_2(n, body):
                body(0, 0, False)
                body(1, 1, False)
                if n > 4:
                    with pool.Fori(1, n // 2 - 1) as i:
                        for e in range(2):
                            body(pool.snap(i * 2 + e), e, False)
                body(n - 2, 0, False)
                body(n - 1, 1, True)

            less = lambda m: m - 1 if isinstance(m, int) else pool.snap(m - 1)
            is0 = lambda m: isinstance(m, int) and m == 0

            low(0, 0, KD)

            def glu(m, e, last):
                low(m * 2 + (S_GLU + 1), 1, KD)
                if is0(m):
                    for name in ("y6", "y7"):
                        copied_wait(pool, name)
                    pool.wait_ge(s5_full, len(fills))
                    memset(acc[:, :], 0.0).then_inc(acc_zero["glu"], 1)
                    memset(vcur[0:CH, 0, :], 0.0)
                    memset(ubuf[:, :, 0:2], 0.0).then_inc(ubuf_zero, 1)
                else:
                    add_square("glu", less(m), 1 - e)
                low(m * 2 + (S_GLU + 2), 0, KD)

            loop_2(KD, glu)
            add_square("glu", KD - 1, 1)

            def up(p, base, before):
                def act_low(m):
                    pool.wait_ge(act_hi_done[p], m + 1)
                    real = {"up0": 0, "up1": META}[p]
                    tt(tile_of(act_lo, m, real), abuf[:, real:L], f32(tile_of(act_hi, m, real)), ALU.subtract
                       ).then_inc(act_lo_done[p], 1)

                def tile(m, e, last):
                    low(m * 2 + (base + 1), 1, KD)
                    if not is0(m):
                        act_low(less(m))
                    low(m * 2 + (base + 2), 0, KS if last else KD)

                loop_2(KF, tile)
                low(base + 2 * KF + 1, 1, KS)
                act_low(KF - 1)

            def distances(half):
                pool.wait_ge(stat_full["glu"], 1)
                if half:
                    pool.wait_ge(acc_done["dn0"], 1)
                d = dint[:, :].rearrange("p (n j) -> p n j", n=NQ)
                part, io = slice(half * CH, (half + 1) * CH), nc.gpsimd.iota
                io(d[part, 0:NCH, 0:BAND], pattern=[[0, NCH], [-1, BAND]], base=CH, channel_multiplier=1)
                io(d[part, 0:NCH, BAND:KEYS], pattern=[[CH, NCH], [-1, META]], base=META, channel_multiplier=1)
                io(d[part, NCH, 0:BAND], pattern=[[-1, BAND]], base=0, channel_multiplier=1)
                io(d[part, NCH, BAND:KEYS], pattern=[[-1, META]], base=0, channel_multiplier=1).then_inc(dint_set, 1)
                pool.wait_ge(dint_set, half + 1)

            def down(p, base, nxt):
                def tile(m, e, last):
                    if is0(m):
                        pool.wait_ge(act_done[{"dn0": "up0", "dn1": "up1"}[p]], KF)
                        pool.wait_ge(stat_full[{"dn0": "glu", "dn1": "o"}[p]], 1)
                        memset(acc[:, :], 0.0).then_inc(acc_zero[p], 1)
                    if not is0(m):
                        low(m * 2 + (base + 1), 1, KS)
                        add_square(p, less(m), 1 - e)
                    if p == "dn0" and isinstance(m, int) and m < 2:
                        distances(m)
                    if not last or nxt:
                        low(m * 2 + (base + 2), 0, nxt if last else KS)

                loop_2(KD, tile)
                add_square(p, KD - 1, 1)

            def attention():
                low(S_KV + 1, 1, KD)
                low(S_KV + 2, 0, KD)
                pool.wait_ge(dist_abs, 1)
                memset(dist[:, 0, 0:CH], FAR)
                memset(dist[:, NCH, 0:BAND], FAR).then_inc(dist_set, 1)
                low(S_KV + 3, 1, KD)
                low(S_Q, 0, KD)
                pool.wait_ge(slab_used, S_Q)
                memset(kcur[:, 0, 0:CH], 0.0)
                memset(kcur[:, NCH, 0:BAND], 0.0)
                memset(qt, 0.0)
                memset(ptm, 0.0)
                memset(vmet, 0.0).then_inc(pads_zero, 1)
                low(S_Q + 1, 1, KD)

                def heads(j, hp, e, ahead):
                    for t in range(GRP):
                        three = slice(GRP * t, GRP * (t + 1))
                        pool.wait_ge(rden_ready, hp * GRP + (t + 1))
                        s = prob[:, e, three, :]
                        rd = rden[:, e, three, None]
                        tt(s[:, :, 0:BAND], s[:, :, 0:BAND], rd.to_broadcast([P, GRP, BAND]), ALU.mult)
                        tt(probm[:, e, three, :], s[:, :, BAND:KEYS], rd.to_broadcast([P, GRP, META]), ALU.mult
                           ).then_inc(p_ready, 1)
                    if ahead:
                        low(hp + (S_Q + 2), e, KD)

                heads(0, 0, 0, True)
                heads(0, 1, 1, True)
                with pool.Fori(1, KVH - 1) as j:
                    for e in range(2):
                        heads(j, pool.snap(j * 2 + e), e, True)
                heads(KVH - 1, HP - 2, 0, True)
                heads(KVH - 1, HP - 1, 1, False)
                pool.wait_ge(stat_full["dn0"], 1)
                memset(acc[:, :], 0.0).then_inc(acc_zero["o"], 1)
                pool.wait_ge(ao_lo_done, HP)
                memset(ubuf[:, :, 0:2], 0.0).then_inc(ubuf_zero, 1)

                def o_tile(m, e, last):
                    low(m + (S_O + 1), 1 - e, KD)
                    if not is0(m):
                        add_square("o", less(m), 1 - e)

                loop_2(KD, o_tile)
                add_square("o", KD - 1, 1)

            up("up0", S_UP0, "glu")
            down("dn0", S_DN0, KD)
            attention()
            up("up1", S_UP1, "o")
            down("dn1", S_DN1, 0)


_INS = ['x', 'meta', 's5_norm', 's5_lambda_re', 's5_lambda_im', 's5_log_step', 's5_b_re', 's5_b_im', 's5_c_re',
        's5_c_im', 's5_d', 's5_w_glu', 'kv_norm', 'w_kv', 'attn_norm', 'w_q', 'sinks', 'w_o', 'ffn_norm', 'ffn_w_up',
        'ffn_conv', 'ffn_w_down', 'final_norm']


def kernel(**inputs):
    import concourse.bacc as bacc
    from concourse.bass_utils import run_bass_kernel_spmd

    nc = bacc.Bacc("TRN2", target_bir_lowering=False, num_devices=1)
    arrays, args = {}, []
    for name in _INS:
        a = np.ascontiguousarray(inputs[name])
        arrays[f"in_{name}"] = a
        args.append(nc.dram_tensor(f"in_{name}", a.shape, mybir.dt.from_np(a.dtype), kind="ExternalInput").ap())
    out = nc.dram_tensor("out", (1, SEQ, D), F32, kind="ExternalOutput").ap()
    k_scratch = nc.dram_tensor("k_scratch", (KVH, HD, L), F32, kind="Internal").ap()
    v_scratch = nc.dram_tensor("v_scratch", (L, KVH * HD), F32, kind="Internal").ap()
    trunk(nc, *args, out, k_scratch, v_scratch)
    r = run_bass_kernel_spmd(nc, [arrays], core_ids=[0])
    return r.results[0]["out"]
```
